# Optimizing a Trainium2 kernel written in Bass

```python
import jax, jax.numpy as jnp
from jax import lax
import numpy as np

D_MODEL = 1024
BATCH = 1
SEQ = 256
DEPTH = 2

D_MIX = D_MODEL
N_MIXERS = 4
D_GROUP = D_MIX // N_MIXERS
HEADS_PER_MIXER = 4
HEAD_DIM = D_GROUP // HEADS_PER_MIXER
POOL_WINDOWS = (2, 4, 8, 16)
CONV_WIDTH = 3
CHUNK = 128
D_FF = 2816
D_IN = D_GROUP * 7
SPLITS = tuple(D_GROUP * i for i in (1, 2, 3, 4, 5, 6))
ALPHA = (2 * DEPTH) ** 0.25
BETA = (8 * DEPTH) ** -0.25
LN_EPS = 1e-5

kernel_name = "hybrid_headgroup_fourier_pool_conv_gmlp_encoder"

def layer_norm(x, g, b):
    xf = x.astype(jnp.float32)
    mu = jnp.mean(xf, axis=-1, keepdims=True)
    var = jnp.mean(jnp.square(xf - mu), axis=-1, keepdims=True)
    return ((xf - mu) * lax.rsqrt(var + LN_EPS) * g + b).astype(x.dtype)

def swiglu_ffn(x, w_gate, w_up, w_down):
    return (jax.nn.silu(x @ w_gate) * (x @ w_up)) @ w_down

def fourier_mixer(a):
    bsz, s, _ = a.shape
    ah = a.astype(jnp.float32).reshape(bsz, s, HEADS_PER_MIXER, HEAD_DIM)
    f = jnp.fft.fftn(ah, axes=(1, 3), norm="ortho").real
    return f.reshape(bsz, s, D_GROUP).astype(a.dtype)

def pool_mixer(p, pool_w, pool_scale):
    bsz, s, _ = p.shape
    pf = p.astype(jnp.float32)
    cs = jnp.concatenate([jnp.zeros((bsz, 1, D_GROUP), jnp.float32), jnp.cumsum(pf, axis=1)], axis=1)
    t = jnp.arange(s)
    outs = []
    for g, w in enumerate(POOL_WINDOWS):
        lo = jnp.clip(t - w // 2, 0, s)
        hi = jnp.clip(t + w - w // 2, 0, s)
        sl = slice(g * HEAD_DIM, (g + 1) * HEAD_DIM)
        c = cs[..., sl]
        win_sum = jnp.take(c, hi, axis=1) - jnp.take(c, lo, axis=1)
        mean = win_sum / (hi - lo).astype(jnp.float32)[None, :, None]
        outs.append(mean - pf[..., sl])
    pooled = jnp.concatenate(outs, axis=-1).astype(p.dtype).reshape(bsz, s, HEADS_PER_MIXER, HEAD_DIM)
    mixed = jnp.einsum('bsgc,gcd->bsgd', pooled, pool_w).reshape(bsz, s, D_GROUP)
    return mixed * pool_scale

def conv_mixer(gate_b, gate_c, h, conv_w):
    s = h.shape[1]
    z = gate_c * h
    pad = CONV_WIDTH // 2
    zp = jnp.pad(z, ((0, 0), (pad, CONV_WIDTH - 1 - pad), (0, 0)))
    y = conv_w[0] * zp[:, 0:s]
    for k in range(1, CONV_WIDTH):
        y = y + conv_w[k] * zp[:, k:k + s]
    return gate_b * y

def gmlp_mixer(u, v, ln_g, ln_b, w_s, b_s):
    bsz, s, _ = v.shape
    vn = layer_norm(v, ln_g, ln_b).reshape(bsz, s // CHUNK, CHUNK, HEADS_PER_MIXER, HEAD_DIM)
    mixed = jnp.einsum('hqk,bnkhd->bnqhd', w_s, vn) + b_s.T[None, None, :, :, None]
    return u * mixed.reshape(bsz, s, D_GROUP)

def headgroup_mixer(x, w_in, pool_w, pool_scale, conv_w, gmlp_ln_g, gmlp_ln_b, gmlp_w_s, gmlp_b_s, w_out):
    proj = x @ w_in
    a, p, gate_b, gate_c, h, u, v = jnp.split(proj, SPLITS, axis=-1)
    y = jnp.concatenate([
        fourier_mixer(a),
        pool_mixer(p, pool_w, pool_scale),
        conv_mixer(gate_b, gate_c, h, conv_w),
        gmlp_mixer(u, v, gmlp_ln_g, gmlp_ln_b, gmlp_w_s, gmlp_b_s),
    ], axis=-1)
    return y @ w_out

def setup_inputs(seed: int = 0) -> dict:
    key = jax.random.key(seed)
    ks = jax.random.split(key, 24)
    L = DEPTH

    def nrm(k, shape, scale):
        return jax.random.normal(k, shape, jnp.float32) * scale

    return {
        "x": nrm(ks[0], (BATCH, SEQ, D_MODEL), 1.0),
        "ffn1_w_gate": nrm(ks[1], (L, D_MODEL, D_FF), D_MODEL ** -0.5),
        "ffn1_w_up": nrm(ks[2], (L, D_MODEL, D_FF), D_MODEL ** -0.5),
        "ffn1_w_down": nrm(ks[3], (L, D_FF, D_MODEL), BETA * D_FF ** -0.5),
        "ln1_g": 1.0 + nrm(ks[4], (L, D_MODEL), 0.05),
        "ln1_b": nrm(ks[5], (L, D_MODEL), 0.02),
        "mix_w_in": nrm(ks[6], (L, D_MODEL, D_IN), D_MODEL ** -0.5),
        "pool_w": nrm(ks[7], (L, HEADS_PER_MIXER, HEAD_DIM, HEAD_DIM), HEAD_DIM ** -0.5),
        "pool_scale": 1.0 + nrm(ks[8], (L, D_GROUP), 0.1),
        "conv_w": nrm(ks[9], (L, CONV_WIDTH, D_GROUP), CONV_WIDTH ** -0.5),
        "gmlp_ln_g": 1.0 + nrm(ks[10], (L, D_GROUP), 0.05),
        "gmlp_ln_b": nrm(ks[11], (L, D_GROUP), 0.02),
        "gmlp_w_s": nrm(ks[12], (L, HEADS_PER_MIXER, CHUNK, CHUNK), CHUNK ** -0.5),
        "gmlp_b_s": 1.0 + nrm(ks[13], (L, HEADS_PER_MIXER, CHUNK), 0.02),
        "mix_w_out": nrm(ks[14], (L, D_MIX, D_MODEL), BETA * D_MIX ** -0.5),
        "ln2_g": 1.0 + nrm(ks[15], (L, D_MODEL), 0.05),
        "ln2_b": nrm(ks[16], (L, D_MODEL), 0.02),
        "ffn2_w_gate": nrm(ks[17], (L, D_MODEL, D_FF), D_MODEL ** -0.5),
        "ffn2_w_up": nrm(ks[18], (L, D_MODEL, D_FF), D_MODEL ** -0.5),
        "ffn2_w_down": nrm(ks[19], (L, D_FF, D_MODEL), BETA * D_FF ** -0.5),
        "ln3_g": 1.0 + nrm(ks[20], (L, D_MODEL), 0.05),
        "ln3_b": nrm(ks[21], (L, D_MODEL), 0.02),
    }

def reference(x, ffn1_w_gate, ffn1_w_up, ffn1_w_down, ln1_g, ln1_b,
              mix_w_in, pool_w, pool_scale, conv_w, gmlp_ln_g, gmlp_ln_b, gmlp_w_s, gmlp_b_s,
              mix_w_out, ln2_g, ln2_b,
              ffn2_w_gate, ffn2_w_up, ffn2_w_down, ln3_g, ln3_b):
    for l in range(DEPTH):
        x = layer_norm(ALPHA * x + 0.5 * swiglu_ffn(x, ffn1_w_gate[l], ffn1_w_up[l], ffn1_w_down[l]),
                       ln1_g[l], ln1_b[l])
        mix = headgroup_mixer(x, mix_w_in[l], pool_w[l], pool_scale[l], conv_w[l],
                              gmlp_ln_g[l], gmlp_ln_b[l], gmlp_w_s[l], gmlp_b_s[l], mix_w_out[l])
        x = layer_norm(ALPHA * x + mix, ln2_g[l], ln2_b[l])
        x = layer_norm(ALPHA * x + 0.5 * swiglu_ffn(x, ffn2_w_gate[l], ffn2_w_up[l], ffn2_w_down[l]),
                       ln3_g[l], ln3_b[l])
    return x


_drawn_inputs = setup_inputs


def setup_inputs(seed=0):
    import zlib

    import numpy as np

    out = dict(_drawn_inputs(seed))
    spreads = {}
    factors = {'pool_scale': 10.966, 'gmlp_ln_g': 17.499, 'gmlp_ln_b': 43.366, 'gmlp_b_s': 22.001}
    for name, (base, spread) in spreads.items():
        noise = np.random.default_rng([zlib.crc32(name.encode()), seed]).standard_normal(out[name].shape)
        drawn = base * np.exp(spread * noise) if base else spread * noise
        out[name] = __import__('jax').numpy.asarray(drawn.astype(out[name].dtype))
    for name, factor in factors.items():
        out[name] = (out[name] * factor).astype(out[name].dtype)
    return out
```

```python
from contextlib import ExitStack

import numpy as np

import concourse.bass as bass
from concourse import mybir

ALU = mybir.AluOpType
ACT = mybir.ActivationFunctionType
F32 = mybir.dt.float32
F32R = mybir.dt.float32r

P = 128
LAYERS = 2
SEQ = 256
D = 1024
DFF = 2816
GROUP = 256
HEADS = 4
HEAD = GROUP // HEADS
CHUNK = 128
WINDOWS = (2, 4, 8, 16)
ALPHA = (2 * LAYERS) ** 0.25
LN_EPS = 1e-5

TT = SEQ // P
KT = D // P
HALF = D // 2
CT = GROUP // P
CHUNKS = DFF // P
W = 1024

MIX_PAIRS = 8
MIX_SINGLES = 6
PAIRS = 2 * CHUNKS + MIX_PAIRS
SINGLES = 2 * CHUNKS + MIX_SINGLES
FFN_PAIR0 = (0, CHUNKS + MIX_PAIRS)
FFN_SINGLE0 = (0, CHUNKS + MIX_SINGLES)
MIX_PAIR0 = CHUNKS
MIX_SINGLE0 = CHUNKS
LAST_SINGLE = (CHUNKS - 1, CHUNKS + MIX_SINGLES - 1, SINGLES - 1)
STAGES = 3
LN_COUNTS = 6
MIX_COUNTS = 21


def build(nc, x, ffn_pairs, ffn_singles, mix_pairs, mix_singles, ln_params, v_params, gate_bias,
          pool_w, small, spatial_w, ident_c, dft_channels, dft_tokens, pool_matrix, out):
    with ExitStack() as ctx:
        def sb(name, shape, dt=F32):
            return ctx.enter_context(nc.sbuf_tensor(name, shape, dt))

        def sem(name):
            return ctx.enter_context(nc.semaphore(name))

        raw_pair = sb("raw_pair", [P, 2, 2 * W])
        raw_single = sb("raw_single", [P, 2, W])
        hi_pair = sb("hi_pair", [P, 2, 2, W], F32R)
        lo_pair = sb("lo_pair", [P, 2, 2, W], F32R)
        hi_single = sb("hi_single", [P, 2, W], F32R)
        lo_single = sb("lo_single", [P, 2, W], F32R)
        x_tok = sb("x_tok", [P, TT, D])
        xT_hi = sb("xT_hi", [P, KT, SEQ], F32R)
        xT_lo = sb("xT_lo", [P, KT, SEQ], F32R)
        res = sb("res", [P, D])
        res_hi = sb("res_hi", [P, TT, D], F32R)
        res_lo = sb("res_lo", [P, TT, D], F32R)
        silu_g = sb("silu_g", [P, 2, SEQ])
        hid = sb("hid", [P, 2, SEQ])
        hid_hi = sb("hid_hi", [P, 2, SEQ], F32R)
        hid_lo = sb("hid_lo", [P, 2, SEQ], F32R)
        centred = sb("centred", [P, 2, HALF])
        stats = sb("stats", [P, 2, 6])
        mean_var = sb("mean_var", [P, 2])
        var_eps = sb("var_eps", [P, 1])
        std = sb("std", [P, 1])
        rstd = sb("rstd", [P, 1])
        ln = sb("ln", [P, 2 * STAGES, D])
        vln = sb("vln", [P, 2, GROUP])
        bias_s = sb("bias_s", [P, CT, CHUNK])
        pool_bd = sb("pool_bd", [P, CT, P])
        chan = sb("chan", [P, 4 * CT])
        ws = sb("ws", [P, HEADS, CHUNK])
        ident = sb("ident", [P, P])
        ident_r = sb("ident_r", [P, P], F32R)
        dft_ch = sb("dft_ch", [P, 2 * P])
        dft_tok = sb("dft_tok", [P, 2, TT, SEQ])
        pool_m = sb("pool_m", [P, HEADS, TT, SEQ])
        aT = sb("aT", [P, CT, SEQ])
        y1 = sb("y1", [P, TT, 2 * GROUP])
        p_tok = sb("p_tok", [P, TT, GROUP])
        pooled = aT
        v_mid = sb("v_mid", [P, GROUP])
        v_tok = sb("v_tok", [P, TT, GROUP])
        c_gate = sb("c_gate", [P, SEQ])
        z_pad = sb("z_pad", [P, SEQ + 2])
        conv = sb("conv", [P, SEQ])
        mixed = sb("mixed", [P, CT, SEQ])
        y_full = sb("y_full", [P, CT, SEQ])
        yT_hi = sb("yT_hi", [P, KT, SEQ], F32R)
        yT_lo = sb("yT_lo", [P, KT, SEQ], F32R)

        acc = ctx.enter_context(nc.psum_tensor("acc", [P, 2 * TT, HALF], F32))
        work = ctx.enter_context(nc.psum_tensor("work", [P, 4, HALF], F32))

        pair_landed = [sem(f"pair_landed{i}") for i in range(2)]
        single_landed = [sem(f"single_landed{i}") for i in range(2)]
        hi_pair_ready, hi_single_ready = sem("hi_pair_ready"), sem("hi_single_ready")
        lo_pair_ready, lo_single_ready = sem("lo_pair_ready"), sem("lo_single_ready")
        pair_used, single_used = sem("pair_used"), sem("single_used")
        x_landed = [sem(f"x_landed{t}") for t in range(TT)]
        x_ready = sem("x_ready")
        transposed = sem("transposed")
        xT_hi_ready, xT_lo_ready = sem("xT_hi_ready"), sem("xT_lo_ready")
        res_step, res_ready = sem("res_step"), sem("res_ready")
        silu_ready, hid_step, hid_ready = sem("silu_ready"), sem("hid_step"), sem("hid_ready")
        acc_done = sem("acc_done")
        ln_step, var_ready, std_ready = sem("ln_step"), sem("var_ready"), sem("std_ready")
        const_landed, ident_landed = sem("const_landed"), sem("ident_landed")
        ident_ready, bd_zeroed, pad_zeroed = sem("ident_ready"), sem("bd_zeroed"), sem("pad_zeroed")
        params_landed = sem("params_landed")
        mix_step = sem("mix_step")
        p_ready, aT_ready, y1_ready = sem("p_ready"), sem("aT_ready"), sem("y1_ready")
        v_var_ready, v_std_ready, v_ready = sem("v_var_ready"), sem("v_std_ready"), sem("v_ready")
        c_ready, z_ready = sem("c_ready"), sem("z_ready")
        dft1_done, pool_done, dft2_done = sem("dft1_done"), sem("pool_done"), sem("dft2_done")
        pooled_ready, pool_w_done, scaled_ready = sem("pooled_ready"), sem("pool_w_done"), sem("scaled_ready")
        spatial_done, mixed_ready = sem("spatial_done"), sem("mixed_ready")
        ya_hi_ready, ya_ready, yb_ready = sem("ya_hi_ready"), sem("ya_ready"), sem("yb_ready")
        yc_ready, yd_ready = sem("yc_ready"), sem("yd_ready")
        stored = sem("stored")
        dve_passed, pool_passed = sem("dve_passed"), sem("pool_passed")

        FREE_PAIR_TILES = 4
        FREE_SINGLES = 2
        PARAM_LOADS = 9
        CONST_LOADS = 3

        def pair_tiles(l, n, i=0):
            return (2 * PAIRS) * l + 2 * n + 4 * i

        def singles(l, n, i=0):
            return SINGLES * l + n + 2 * i

        def pair_loads(l, n, i=0):
            return (PAIRS // 2) * l + n // 2 + i

        def single_loads(l, n, i=0):
            return (SINGLES // 2) * l + n // 2 + i

        block = ctx.enter_context(nc.Block())

        @block.sync
        def _(sp):
            def load_pair(l, n, src, i=0):
                sp.wait_ge(lo_pair_ready, pair_tiles(l, n, i) - 2 + FREE_PAIR_TILES)
                sp.dma_start(raw_pair[:, n % 2, :], src).then_inc(pair_landed[n % 2], 16)

            def load_single(l, n, src, i=0):
                sp.wait_ge(lo_single_ready, singles(l, n, i) - 1 + FREE_SINGLES)
                sp.dma_start(raw_single[:, n % 2, :], src).then_inc(single_landed[n % 2], 16)

            def ffn_pair(l, f, j, i=0):
                load_pair(l, FFN_PAIR0[f] + j, ffn_pairs[f, (l * CHUNKS + j) + 2 * i], i)

            def ffn_single(l, f, j, i=0):
                load_single(l, FFN_SINGLE0[f] + j, ffn_singles[f, (l * CHUNKS + j) + 2 * i], i)

            def mix_pair(l, g):
                load_pair(l, MIX_PAIR0 + g, mix_pairs[l * MIX_PAIRS + g])

            def mix_single(l, g):
                load_single(l, MIX_SINGLE0 + g, mix_singles[l * MIX_SINGLES + g])

            for t in range(TT):
                sp.dma_start(x_tok[:, t, :], x[t * P:(t + 1) * P, :]).then_inc(x_landed[t], 16)
            with sp.Fori(0, LAYERS) as l:
                ffn_pair(l, 0, 0)
                ffn_pair(l, 0, 1)
                ffn_single(l, 0, 0)
                with sp.Fori(0, (CHUNKS - 2) // 2) as i:
                    for j in (0, 1):
                        ffn_pair(l, 0, j + 2, i)
                        ffn_single(l, 0, j + 1, i)
                mix_pair(l, 0)
                ffn_single(l, 0, CHUNKS - 1)
                mix_pair(l, 1)
                mix_single(l, 0)
                mix_single(l, 1)
                for g in (2, 3, 4, 5):
                    mix_pair(l, g)
                mix_single(l, 2)
                mix_pair(l, 6)
                mix_single(l, 3)
                mix_pair(l, 7)
                mix_single(l, 4)
                mix_single(l, 5)
                ffn_pair(l, 1, 0)
                ffn_pair(l, 1, 1)
                ffn_single(l, 1, 0)
                with sp.Fori(0, (CHUNKS - 2) // 2) as i:
                    for j in (0, 1):
                        ffn_pair(l, 1, j + 2, i)
                        ffn_single(l, 1, j + 1, i)
                ffn_single(l, 1, CHUNKS - 1)
            for t in range(TT):
                sp.wait_ge(x_ready, 2 * TT * (STAGES * LAYERS) + 2 * (t + 1))
                sp.dma_start(out[t * P:(t + 1) * P, :], x_tok[:, t, :]).then_inc(stored, 16)
            sp.wait_ge(stored, 16 * TT)

        @block.gpsimd
        def _(pool):
            pool.dma_start(ident[:, :], ident_c).then_inc(ident_landed, 16)
            nc.gpsimd.memset(pool_bd[:, :, :], 0.0).then_inc(bd_zeroed, 1)
            nc.gpsimd.memset(z_pad[:, :], 0.0).then_inc(pad_zeroed, 1)
            pool.wait_ge(bd_zeroed, 1)
            pool.dma_start(dft_ch[:, :], dft_channels).then_inc(const_landed, 16)
            pool.dma_start(dft_tok[:, :, :, :], dft_tokens).then_inc(const_landed, 16)
            pool.dma_start(pool_m[:, :, :, :], pool_matrix).then_inc(const_landed, 16)

            def residual(l, s):
                scale = ALPHA if s == 1 else 2 * ALPHA
                for t in range(TT):
                    n = TT * STAGES * l + TT * s + t
                    pool.wait_ge(x_ready, 2 * n + 2)
                    if t > 0:
                        pool.wait_ge(res_ready, n)
                    nc.gpsimd.sem_inc(pool_passed, 1)
                    nc.gpsimd.tensor_scalar(res[:, :], x_tok[:, t, :], scale, 0.0, ALU.mult, ALU.add)\
                        .then_inc(res_step, 1)
                    pool.wait_ge(res_step, 2 * n + 1)
                    nc.gpsimd.sem_inc(pool_passed, 1)
                    nc.gpsimd.tensor_scalar(res_hi[:, t, :], res[:, :], 1.0, 0.0, ALU.mult, ALU.add)\
                        .then_inc(res_step, 1)
                    pool.wait_ge(res_step, 2 * n + 2)
                    nc.gpsimd.tensor_tensor(res_lo[:, t, :], res[:, :], res_hi[:, t, :].bitcast(F32),
                                            ALU.subtract).then_inc(res_ready, 1)

            with pool.Fori(0, LAYERS) as l:
                residual(l, 0)
                pool.dma_start(ln[:, :, :], ln_params[l].partition_broadcast(P)).then_inc(params_landed, 16)
                pool.dma_start(vln[:, :, :], v_params[l].partition_broadcast(P)).then_inc(params_landed, 16)
                for hh in range(2):
                    at = slice(hh * HEAD, (hh + 1) * HEAD)
                    pool.dma_start(bias_s[at, :, :], gate_bias[l, hh].partition_broadcast(HEAD))\
                        .then_inc(params_landed, 16)
                    pool.dma_start(pool_bd[at, :, at], pool_w[l, hh]).then_inc(params_landed, 16)
                pool.dma_start(chan[:, :], small[l]).then_inc(params_landed, 16)
                pool.dma_start(ws[:, 0:2, :], spatial_w[l, :, 0:2, :]).then_inc(params_landed, 16)
                pool.dma_start(ws[:, 2:4, :], spatial_w[l, :, 2:4, :]).then_inc(params_landed, 16)
                residual(l, 1)
                residual(l, 2)

        @block.scalar
        def _(act):
            def copy(dst, src):
                return nc.scalar.activation(dst, src, ACT.Copy)

            def hi_of_pair(l, n, i=0):
                act.wait_ge(pair_landed[n % 2], 16 * pair_loads(l, n, i) + 16)
                for a in range(2):
                    act.wait_ge(pair_used, pair_tiles(l, n, i) - 3 + a + FREE_PAIR_TILES)
                    copy(hi_pair[:, n % 2, a, :], raw_pair[:, n % 2, a * W:(a + 1) * W])\
                        .then_inc(hi_pair_ready, 1)

            def hi_of_single(l, n, i=0):
                act.wait_ge(single_landed[n % 2], 16 * single_loads(l, n, i) + 16)
                act.wait_ge(single_used, singles(l, n, i) - 1 + FREE_SINGLES)
                copy(hi_single[:, n % 2, :], raw_single[:, n % 2, :]).then_inc(hi_single_ready, 1)

            def spread(l, s):
                for t in range(TT):
                    for h in range(2):
                        n = 2 * TT * STAGES * l + 2 * TT * s + 2 * t + h
                        act.wait_ge(transposed, n + 1)
                        copy(xT_hi[:, 4 * h:4 * h + 4, t * P:(t + 1) * P],
                             work[:, 2 * t + h, :].rearrange("p (k n) -> p k n", k=4)).then_inc(xT_hi_ready, 1)

            def norm(l, s):
                for t in range(TT):
                    n = TT * STAGES * l + TT * s + t
                    act.wait_ge(var_ready, n + 1)
                    nc.scalar.activation(std[:, :], var_eps[:, :], ACT.Sqrt).then_inc(std_ready, 1)

            def silu(l, f, j, i=0):
                act.wait_ge(pair_used, pair_tiles(l, FFN_PAIR0[f] + j, i) + 1 + FREE_PAIR_TILES)
                nc.scalar.activation(silu_g[:, j % 2, :], work[:, 2 * (j % 2), 0:SEQ], ACT.Silu)\
                    .then_inc(silu_ready, 1)

            def ffn(l, f, after_20, after_21):
                def step(j, i=0):
                    silu(l, f, j, i)
                    hi_of_pair(l, FFN_PAIR0[f] + j + 2, i)
                    hi_of_single(l, FFN_SINGLE0[f] + j + 1, i)

                step(0)
                with act.Fori(0, 9) as i:
                    step(1, i)
                    step(2, i)
                step(19)
                silu(l, f, 20)
                after_20()
                silu(l, f, 21)
                after_21()

            act.wait_ge(ident_landed, 16)
            copy(ident_r[:, :], ident[:, :]).then_inc(ident_ready, 1)
            with act.Fori(0, LAYERS) as l:
                spread(l, 0)
                hi_of_pair(l, 0)
                hi_of_pair(l, 1)
                hi_of_single(l, 0)

                def mix_pair(g):
                    hi_of_pair(l, MIX_PAIR0 + g)

                def mix_single(g):
                    hi_of_single(l, MIX_SINGLE0 + g)

                def into_mixer_20():
                    mix_pair(0)
                    hi_of_single(l, CHUNKS - 1)

                def into_mixer_21():
                    mix_pair(1)
                    mix_single(0)

                def to_end_20():
                    hi_of_single(l, FFN_SINGLE0[1] + CHUNKS - 1)

                ffn(l, 0, into_mixer_20, into_mixer_21)
                norm(l, 0)
                spread(l, 1)

                mix_single(1)
                mix_pair(2)
                mix_pair(3)
                for t in range(TT):
                    act.wait_ge(pair_used, pair_tiles(l, MIX_PAIR0 + 2) + FREE_PAIR_TILES)
                    copy(p_tok[:, t, :], acc[:, t, 0:GROUP]).then_inc(p_ready, 1)
                for t in range(TT):
                    act.wait_ge(v_var_ready, TT * l + t + 1)
                    nc.scalar.activation(std[:, :], var_eps[:, :], ACT.Sqrt).then_inc(v_std_ready, 1)
                act.wait_ge(pair_used, pair_tiles(l, MIX_PAIR0 + 3) + FREE_PAIR_TILES)
                copy(aT[:, :, :], work[:, 0, :].rearrange("p (c n) -> p c n", c=CT)).then_inc(aT_ready, 1)
                mix_pair(4)
                act.wait_ge(pair_used, pair_tiles(l, MIX_PAIR0 + 4) + FREE_PAIR_TILES)
                copy(c_gate[:, :], work[:, 1, 0:SEQ]).then_inc(c_ready, 1)
                mix_pair(5)
                for t in range(TT):
                    act.wait_ge(dft1_done, TT * l + t + 1)
                    copy(y1[:, t, :], acc[:, TT + t, :]).then_inc(y1_ready, 1)
                mix_single(2)
                act.wait_ge(pair_used, pair_tiles(l, MIX_PAIR0 + 5) + FREE_PAIR_TILES)
                act.wait_ge(z_ready, CT * l + 1)
                copy(c_gate[:, :], work[:, 3, 0:SEQ]).then_inc(c_ready, 1)
                mix_pair(6)
                act.wait_ge(pool_done, l + 1)
                copy(pooled[:, :, :], work[:, 0, :].rearrange("p (c n) -> p c n", c=CT))\
                    .then_inc(pooled_ready, 1)
                mix_single(3)
                act.wait_ge(dft2_done, l + 1)
                copy(yT_hi[:, 0:2, :], acc[:, 1, :].rearrange("p (c n) -> p c n", c=CT))\
                    .then_inc(ya_hi_ready, 1)
                mix_pair(7)
                act.wait_ge(pool_w_done, l + 1)
                act.wait_ge(yc_ready, CT * l + CT)
                for c in range(CT):
                    nc.scalar.activation(y_full[:, c, :], work[:, 3, c * SEQ:(c + 1) * SEQ], ACT.Copy,
                                         scale=chan[:, c:c + 1]).then_inc(scaled_ready, 1)
                mix_single(4)
                mix_single(5)
                hi_of_pair(l, FFN_PAIR0[1])
                hi_of_pair(l, FFN_PAIR0[1] + 1)
                hi_of_single(l, FFN_SINGLE0[1])
                norm(l, 1)

                spread(l, 2)
                ffn(l, 1, to_end_20, lambda: None)
                norm(l, 2)

        @block.vector
        def _(dve):
            def lo_of_pair(l, n, i=0):
                for a in range(2):
                    dve.wait_ge(hi_pair_ready, pair_tiles(l, n, i) + a + 1)
                    nc.vector.tensor_tensor(lo_pair[:, n % 2, a, :], raw_pair[:, n % 2, a * W:(a + 1) * W],
                                            hi_pair[:, n % 2, a, :].bitcast(F32), ALU.subtract)\
                        .then_inc(lo_pair_ready, 1)

            def lo_of_single(l, n, i=0):
                dve.wait_ge(hi_single_ready, singles(l, n, i) + 1)
                nc.vector.tensor_tensor(lo_single[:, n % 2, :], raw_single[:, n % 2, :],
                                        hi_single[:, n % 2, :].bitcast(F32), ALU.subtract)\
                    .then_inc(lo_single_ready, 1)

            def spread(l, s):
                for t in range(TT):
                    for h in range(2):
                        n = 2 * TT * STAGES * l + 2 * TT * s + 2 * t + h
                        dve.wait_ge(xT_hi_ready, n + 1)
                        at = (slice(None), slice(4 * h, 4 * h + 4), slice(t * P, (t + 1) * P))
                        nc.vector.tensor_tensor(xT_lo[at],
                                                work[:, 2 * t + h, :].rearrange("p (k n) -> p k n", k=4),
                                                xT_hi[at].bitcast(F32), ALU.subtract).then_inc(xT_lo_ready, 1)

            def norm(l, s):
                eps = LN_EPS if s == 1 else 4 * LN_EPS
                for t in range(TT):
                    n = TT * STAGES * l + TT * s + t
                    step = LN_COUNTS * n
                    if t == 0:
                        dve.wait_ge(acc_done, STAGES * l + s + 1)
                    else:
                        dve.wait_ge(single_used, singles(l, LAST_SINGLE[s]) + 1 + FREE_SINGLES)
                    for h in range(2):
                        nc.vector.bn_stats(stats[:, h, :], acc[:, 2 * t + h, :]).then_inc(ln_step, 1)
                    dve.wait_ge(ln_step, step + 2)
                    nc.vector.sem_inc(dve_passed, 1)
                    nc.vector.bn_aggr(mean_var[:, :], stats[:, :, :].rearrange("p a b -> p (a b)"))\
                        .then_inc(ln_step, 1)
                    dve.wait_ge(ln_step, step + 3)
                    nc.vector.tensor_scalar_add(var_eps[:, :], mean_var[:, 1:2], eps).then_inc(var_ready, 1)
                    if s == 0 and t == 0:
                        dve.wait_ge(params_landed, 16 * PARAM_LOADS * (l + 1))
                    for h in range(2):
                        cols = slice(h * HALF, (h + 1) * HALF)
                        nc.vector.scalar_tensor_tensor(centred[:, h, :], acc[:, 2 * t + h, :], mean_var[:, 0:1],
                                                       ln[:, 2 * s, cols], ALU.subtract, ALU.mult)\
                            .then_inc(ln_step, 1)
                        if h == 0:
                            dve.wait_ge(std_ready, n + 1)
                            nc.vector.reciprocal(rstd[:, :], std[:, :]).then_inc(ln_step, 1)
                    for h in range(2):
                        cols = slice(h * HALF, (h + 1) * HALF)
                        dve.wait_ge(ln_step, step + 6)
                        nc.vector.scalar_tensor_tensor(x_tok[:, t, cols], centred[:, h, :], rstd[:, :],
                                                       ln[:, 2 * s + 1, cols], ALU.mult, ALU.add)\
                            .then_inc(x_ready, 1)

            def hidden(l, f, j, i=0):
                n = 2 * CHUNKS * l + CHUNKS * f + j + 2 * i
                dve.wait_ge(pair_used, pair_tiles(l, FFN_PAIR0[f] + j, i) + 2 + FREE_PAIR_TILES)
                dve.wait_ge(silu_ready, n + 1)
                b = j % 2
                up = work[:, 2 * b + 1, 0:SEQ]
                nc.vector.tensor_tensor(hid[:, b, :], silu_g[:, b, :], up, ALU.mult).then_inc(hid_step, 1)
                dve.wait_ge(hid_step, 2 * n + 1)
                nc.vector.tensor_copy(hid_hi[:, b, :], hid[:, b, :]).then_inc(hid_step, 1)
                dve.wait_ge(hid_step, 2 * n + 2)
                nc.vector.tensor_tensor(hid_lo[:, b, :], hid[:, b, :], hid_hi[:, b, :].bitcast(F32),
                                        ALU.subtract).then_inc(hid_ready, 1)

            def ffn(l, f, after_20, after_21):
                def step(j, i=0):
                    hidden(l, f, j, i)
                    lo_of_pair(l, FFN_PAIR0[f] + j + 2, i)
                    lo_of_single(l, FFN_SINGLE0[f] + j + 1, i)

                step(0)
                with dve.Fori(0, 9) as i:
                    step(1, i)
                    step(2, i)
                step(19)
                hidden(l, f, 20)
                after_20()
                hidden(l, f, 21)
                after_21()

            nc.vector.sem_inc(lo_pair_ready, FREE_PAIR_TILES)
            nc.vector.sem_inc(lo_single_ready, FREE_SINGLES)
            for t in range(TT):
                dve.wait_ge(x_landed[t], 16)
                nc.vector.sem_inc(x_ready, 2)
            dve.wait_ge(pad_zeroed, 1)

            with dve.Fori(0, LAYERS) as l:
                spread(l, 0)
                lo_of_pair(l, 0)
                lo_of_pair(l, 1)
                lo_of_single(l, 0)

                def mix_pair(g):
                    lo_of_pair(l, MIX_PAIR0 + g)

                def mix_single(g):
                    lo_of_single(l, MIX_SINGLE0 + g)

                def into_mixer_20():
                    mix_pair(0)
                    lo_of_single(l, CHUNKS - 1)

                def into_mixer_21():
                    mix_pair(1)
                    mix_single(0)

                def to_end_20():
                    lo_of_single(l, FFN_SINGLE0[1] + CHUNKS - 1)

                ffn(l, 0, into_mixer_20, into_mixer_21)
                norm(l, 0)
                spread(l, 1)

                count = [0]

                def chain(ins):
                    count[0] += 1
                    ins.then_inc(mix_step, 1)
                    dve.wait_ge(mix_step, MIX_COUNTS * l + count[0])

                mix_single(1)
                mix_pair(2)
                mix_pair(3)
                dve.wait_ge(pair_used, pair_tiles(l, MIX_PAIR0 + 2) + FREE_PAIR_TILES)
                for t in range(TT):
                    dve.wait_ge(p_ready, TT * l + t + 1)
                    v = acc[:, t, GROUP:2 * GROUP]
                    chain(nc.vector.bn_stats(stats[:, 0, :], v))
                    nc.vector.sem_inc(dve_passed, 1)
                    chain(nc.vector.bn_aggr(mean_var[:, :], stats[:, 0, :]))
                    nc.vector.tensor_scalar_add(var_eps[:, :], mean_var[:, 1:2], LN_EPS).then_inc(v_var_ready, 1)
                    chain(nc.vector.scalar_tensor_tensor(v_mid[:, :], v, mean_var[:, 0:1], vln[:, 0, :],
                                                         ALU.subtract, ALU.mult))
                    dve.wait_ge(v_std_ready, TT * l + t + 1)
                    chain(nc.vector.reciprocal(rstd[:, :], std[:, :]))
                    nc.vector.scalar_tensor_tensor(v_tok[:, t, :], v_mid[:, :], rstd[:, :], vln[:, 1, :],
                                                   ALU.mult, ALU.add).then_inc(v_ready, 1)
                mix_pair(4)

                def conv_group(c, h_at, b_at):
                    dve.wait_ge(c_ready, CT * l + c + 1)
                    nc.vector.tensor_tensor(z_pad[:, 1:SEQ + 1], c_gate[:, :], h_at, ALU.mult).then_inc(z_ready, 1)
                    dve.wait_ge(z_ready, CT * l + c + 1)

                    def w(k):
                        return chan[:, CT * (k + 1) + c:CT * (k + 1) + c + 1]

                    chain(nc.vector.tensor_scalar(conv[:, :], z_pad[:, 0:SEQ], w(0), None, ALU.mult))
                    for k in (1, 2):
                        chain(nc.vector.scalar_tensor_tensor(conv[:, :], z_pad[:, k:k + SEQ], w(k), conv[:, :],
                                                             ALU.mult, ALU.add))
                    dve.wait_ge(single_used, singles(l, MIX_SINGLE0 + c) + 1 + FREE_SINGLES)
                    chain(nc.vector.tensor_tensor(y_full[:, c, :], conv[:, :], b_at, ALU.mult))
                    chain(nc.vector.tensor_copy(yT_hi[:, 4 + c, :], y_full[:, c, :]))
                    nc.vector.tensor_tensor(yT_lo[:, 4 + c, :], y_full[:, c, :], yT_hi[:, 4 + c, :].bitcast(F32),
                                            ALU.subtract).then_inc(yc_ready, 1)

                conv_group(0, work[:, 1, SEQ:2 * SEQ], work[:, 2, 0:SEQ])
                mix_pair(5)
                mix_single(2)
                conv_group(1, work[:, 3, SEQ:2 * SEQ], work[:, 2, SEQ:2 * SEQ])
                mix_pair(6)
                dve.wait_ge(spatial_done, l + 1)
                for c in range(CT):
                    last = nc.vector.tensor_tensor(
                        mixed[:, c, :].rearrange("p (t q) -> p t q", t=TT),
                        acc[:, 0, c * SEQ:(c + 1) * SEQ].rearrange("p (t q) -> p t q", t=TT),
                        bias_s[:, c, :].unsqueeze(1).to_broadcast([P, TT, CHUNK]), ALU.add)
                    last.then_inc(mixed_ready, 1)
                mix_single(3)
                dve.wait_ge(ya_hi_ready, l + 1)
                nc.vector.tensor_tensor(yT_lo[:, 0:2, :], acc[:, 1, :].rearrange("p (c n) -> p c n", c=CT),
                                        yT_hi[:, 0:2, :].bitcast(F32), ALU.subtract).then_inc(ya_ready, 1)
                mix_pair(7)
                dve.wait_ge(scaled_ready, CT * (l + 1))
                chain(nc.vector.tensor_copy(yT_hi[:, 2:4, :], y_full[:, :, :]))
                nc.vector.tensor_tensor(yT_lo[:, 2:4, :], y_full[:, :, :], yT_hi[:, 2:4, :].bitcast(F32),
                                        ALU.subtract).then_inc(yb_ready, 1)
                mix_single(4)
                dve.wait_ge(pair_used, pair_tiles(l, MIX_PAIR0 + 6) + FREE_PAIR_TILES)
                dve.wait_ge(mixed_ready, CT * (l + 1))
                dve.wait_ge(yb_ready, l + 1)
                chain(nc.vector.tensor_tensor(y_full[:, :, :], mixed[:, :, :],
                                              work[:, 1, :].rearrange("p (c n) -> p c n", c=CT), ALU.mult))
                chain(nc.vector.tensor_copy(yT_hi[:, 6:8, :], y_full[:, :, :]))
                nc.vector.tensor_tensor(yT_lo[:, 6:8, :], y_full[:, :, :], yT_hi[:, 6:8, :].bitcast(F32),
                                        ALU.subtract).then_inc(yd_ready, 1)
                assert count[0] == MIX_COUNTS, count
                mix_single(5)
                lo_of_pair(l, FFN_PAIR0[1])
                lo_of_pair(l, FFN_PAIR0[1] + 1)
                lo_of_single(l, FFN_SINGLE0[1])
                norm(l, 1)

                spread(l, 2)
                ffn(l, 1, to_end_20, lambda: None)
                norm(l, 2)

        @block.tensor
        def _(pe):
            def exact(dst, w_hi, w_lo, m_hi, m_lo, first, last):
                nc.tensor.matmul(dst, w_hi, m_hi, start=first, stop=False)
                nc.tensor.matmul(dst, w_hi, m_lo, start=False, stop=False)
                return nc.tensor.matmul(dst, w_lo, m_hi, start=False, stop=last)

            def spread(l, s):
                for t in range(TT):
                    for h in range(2):
                        n = 2 * TT * STAGES * l + 2 * TT * s + 2 * t + h
                        pe.wait_ge(x_ready, n + 1)
                        for k in range(4):
                            col = h * HALF + k * P
                            last = nc.tensor.transpose(work[:, 2 * t + h, k * P:(k + 1) * P],
                                                       x_tok[:, t, col:col + P], ident[:, :])
                        last.then_inc(transposed, 1)
                pe.wait_ge(xT_lo_ready, 2 * TT * STAGES * l + 2 * TT * (s + 1))

            def residual(l, s):
                for t in range(TT):
                    pe.wait_ge(res_ready, TT * STAGES * l + TT * s + t + 1)
                    for h in range(2):
                        cols = slice(h * HALF, (h + 1) * HALF)
                        nc.tensor.matmul(acc[:, 2 * t + h, :], ident_r[:, :], res_hi[:, t, cols],
                                         start=True, stop=False)
                        nc.tensor.matmul(acc[:, 2 * t + h, :], ident_r[:, :], res_lo[:, t, cols],
                                         start=False, stop=False)

            def channels_major(l, n, a, dst, i=0):
                pe.wait_ge(lo_pair_ready, pair_tiles(l, n, i) + a + 1 + FREE_PAIR_TILES)
                for k in range(KT):
                    at = slice(k * P, (k + 1) * P)
                    last = exact(dst, hi_pair[:, n % 2, a, at], lo_pair[:, n % 2, a, at],
                                 xT_hi[:, k, :], xT_lo[:, k, :], k == 0, k == KT - 1)
                last.then_inc(pair_used, 1)

            def gate_up(l, f, j, i=0):
                channels_major(l, FFN_PAIR0[f] + j, 0, work[:, 2 * (j % 2), 0:SEQ], i)
                channels_major(l, FFN_PAIR0[f] + j, 1, work[:, 2 * (j % 2) + 1, 0:SEQ], i)

            def down(l, f, j, i=0, final=False):
                n = FFN_SINGLE0[f] + j
                pe.wait_ge(lo_single_ready, singles(l, n, i) + 1 + FREE_SINGLES)
                pe.wait_ge(hid_ready, 2 * CHUNKS * l + CHUNKS * f + j + 2 * i + 1)
                to_output(n % 2, hid_hi[:, j % 2, :], hid_lo[:, j % 2, :], hi_single[:, n % 2, :],
                          lo_single[:, n % 2, :], final).then_inc(single_used, 1)

            def to_output(b, y_hi, y_lo, w_hi, w_lo, final):
                for t in range(TT):
                    toks = slice(t * P, (t + 1) * P)
                    for h in range(2):
                        cols = slice(h * HALF, (h + 1) * HALF)
                        last = exact(acc[:, 2 * t + h, :], y_hi[:, toks], y_lo[:, toks], w_hi[:, cols],
                                     w_lo[:, cols], False, final)
                    if final and t == 0:
                        last.then_inc(acc_done, 1)
                return last

            def ffn(l, f):
                s = 2 * f
                gate_up(l, f, 0)
                gate_up(l, f, 1)
                residual(l, s)
                down(l, f, 0)
                with pe.Fori(0, (CHUNKS - 2) // 2) as i:
                    for j in (2, 3):
                        gate_up(l, f, j, i)
                        down(l, f, j - 1, i)
                down(l, f, CHUNKS - 1, final=True)

            nc.tensor.sem_inc(pair_used, FREE_PAIR_TILES)
            nc.tensor.sem_inc(single_used, FREE_SINGLES)
            pe.wait_ge(ident_landed, 16)
            pe.wait_ge(ident_ready, 1)
            with pe.Fori(0, LAYERS) as l:
                spread(l, 0)
                ffn(l, 0)
                spread(l, 1)

                for g in range(2):
                    n = MIX_PAIR0 + g
                    for a in range(2):
                        pe.wait_ge(lo_pair_ready, pair_tiles(l, n) + a + 1 + FREE_PAIR_TILES)
                        for t in range(TT):
                            toks = slice(t * P, (t + 1) * P)
                            for kk in range(2):
                                k = 4 * g + 2 * a + kk
                                at = slice(kk * HALF, (kk + 1) * HALF)
                                last = exact(acc[:, t, :], xT_hi[:, k, toks], xT_lo[:, k, toks],
                                             hi_pair[:, n % 2, a, at], lo_pair[:, n % 2, a, at],
                                             k == 0, k == KT - 1)
                        last.then_inc(pair_used, 1)
                for c in range(CT):
                    channels_major(l, MIX_PAIR0 + 2, c, work[:, 0, c * SEQ:(c + 1) * SEQ])

                def gate_b(c):
                    n = MIX_SINGLE0 + c
                    pe.wait_ge(lo_single_ready, singles(l, n) + 1 + FREE_SINGLES)
                    for k in range(KT):
                        at = slice(k * P, (k + 1) * P)
                        last = exact(work[:, 2, c * SEQ:(c + 1) * SEQ], hi_single[:, n % 2, at],
                                     lo_single[:, n % 2, at], xT_hi[:, k, :], xT_lo[:, k, :],
                                     k == 0, k == KT - 1)
                    last.then_inc(single_used, 1)

                channels_major(l, MIX_PAIR0 + 3, 0, work[:, 1, 0:SEQ])
                channels_major(l, MIX_PAIR0 + 3, 1, work[:, 1, SEQ:2 * SEQ])
                gate_b(0)
                pe.wait_ge(const_landed, 16 * CONST_LOADS)
                pe.wait_ge(aT_ready, l + 1)
                for t in range(TT):
                    for c in range(CT):
                        last = nc.tensor.matmul(acc[:, TT + t, c * 2 * P:(c + 1) * 2 * P],
                                                aT[:, c, t * P:(t + 1) * P], dft_ch[:, :], start=True, stop=True)
                    last.then_inc(dft1_done, 1)
                channels_major(l, MIX_PAIR0 + 4, 0, work[:, 3, 0:SEQ])
                channels_major(l, MIX_PAIR0 + 4, 1, work[:, 3, SEQ:2 * SEQ])
                pe.wait_ge(yc_ready, CT * l + 1)
                gate_b(1)
                pe.wait_ge(p_ready, TT * (l + 1))
                for g in range(HEADS):
                    dst = work[(g % 2) * HEAD:(g % 2 + 1) * HEAD, 0, (g // 2) * SEQ:(g // 2 + 1) * SEQ]
                    for t in range(TT):
                        last = nc.tensor.matmul(dst, p_tok[:, t, g * HEAD:(g + 1) * HEAD], pool_m[:, g, t, :],
                                                start=(t == 0), stop=(t == TT - 1))
                last.then_inc(pool_done, 1)
                pe.wait_ge(v_ready, TT * (l + 1))
                pe.wait_ge(params_landed, 16 * PARAM_LOADS * (l + 1))
                for g in range(HEADS):
                    for t in range(TT):
                        col = (g // 2) * SEQ + t * P
                        dst = acc[(g % 2) * HEAD:(g % 2 + 1) * HEAD, 0, col:col + P]
                        last = nc.tensor.matmul(dst, v_tok[:, t, g * HEAD:(g + 1) * HEAD], ws[:, g, :],
                                                start=True, stop=True)
                last.then_inc(spatial_done, 1)
                pe.wait_ge(y1_ready, TT * (l + 1))
                for c in range(CT):
                    for t in range(TT):
                        for part in range(2):
                            col = c * 2 * P + part * P
                            last = nc.tensor.matmul(acc[:, 1, c * SEQ:(c + 1) * SEQ], y1[:, t, col:col + P],
                                                    dft_tok[:, part, t, :], start=(t == 0 and part == 0),
                                                    stop=(t == TT - 1 and part == 1))
                last.then_inc(dft2_done, 1)
                pe.wait_ge(z_ready, CT * l + 1)
                for c in range(CT):
                    channels_major(l, MIX_PAIR0 + 5, c, work[:, 1, c * SEQ:(c + 1) * SEQ])
                pe.wait_ge(pooled_ready, l + 1)
                pe.wait_ge(z_ready, CT * (l + 1))
                for c in range(CT):
                    last = nc.tensor.matmul(work[:, 3, c * SEQ:(c + 1) * SEQ], pool_bd[:, c, :],
                                            pooled[:, c, :], start=True, stop=True)
                last.then_inc(pool_w_done, 1)
                pe.wait_ge(mixed_ready, CT * (l + 1))
                pe.wait_ge(ya_ready, l + 1)
                residual(l, 1)

                def out_pair(g, k0):
                    n = MIX_PAIR0 + g
                    for a in range(2):
                        pe.wait_ge(lo_pair_ready, pair_tiles(l, n) + a + 1 + FREE_PAIR_TILES)
                        to_output(0, yT_hi[:, k0 + a, :], yT_lo[:, k0 + a, :], hi_pair[:, n % 2, a, :],
                                  lo_pair[:, n % 2, a, :], False).then_inc(pair_used, 1)

                def out_single(g, k, final=False):
                    n = MIX_SINGLE0 + g
                    pe.wait_ge(lo_single_ready, singles(l, n) + 1 + FREE_SINGLES)
                    to_output(0, yT_hi[:, k, :], yT_lo[:, k, :], hi_single[:, n % 2, :],
                              lo_single[:, n % 2, :], final).then_inc(single_used, 1)

                out_pair(6, 0)
                pe.wait_ge(yc_ready, CT * (l + 1))
                out_single(2, 4)
                out_single(3, 5)
                pe.wait_ge(yb_ready, l + 1)
                out_pair(7, 2)
                pe.wait_ge(yd_ready, l + 1)
                out_single(4, 6)
                out_single(5, 7, final=True)

                spread(l, 2)
                ffn(l, 1)


def constants():
    n = np.arange(HEAD)
    ang = 2 * np.pi * np.outer(n, n) / HEAD
    ch = np.zeros((P, 2, 2, HEAD))
    for hh in range(2):
        ch[hh * HEAD:(hh + 1) * HEAD, 0, hh] = np.cos(ang)
        ch[hh * HEAD:(hh + 1) * HEAD, 1, hh] = np.sin(ang)
    ch = ch.reshape(P, 2 * P) / np.sqrt(HEAD)
    n = np.arange(SEQ)
    ang = 2 * np.pi * (np.outer(n, n) % SEQ) / SEQ
    tok = np.stack([np.cos(ang), -np.sin(ang)]) / np.sqrt(SEQ)
    tok = tok.reshape(2, TT, P, SEQ).transpose(2, 0, 1, 3)
    pool = np.zeros((HEADS, SEQ, SEQ))
    for g, w in enumerate(WINDOWS):
        for t in range(SEQ):
            lo, hi = max(t - w // 2, 0), min(t + w - w // 2, SEQ)
            pool[g, lo:hi, t] = 1.0 / (hi - lo)
            pool[g, t, t] -= 1.0
    pool = pool.reshape(HEADS, TT, P, SEQ).transpose(2, 0, 1, 3)
    return {"ident": np.eye(P), "dft_channels": ch, "dft_tokens": tok, "pool_matrix": pool}


def kernel(**inputs):
    import concourse.bacc as bacc
    from concourse.bass_utils import run_bass_kernel_spmd as run

    a = {k: np.asarray(v) for k, v in inputs.items()}
    L, C = LAYERS, CHUNKS

    def columns(w, tile):
        n = w.shape[2] // tile
        return w.reshape(L, KT, P, n, tile).transpose(0, 3, 2, 1, 4)

    def ffn_pairs(n):
        gate = columns(a[f"ffn{n}_w_gate"], P).reshape(L * C, P, W)
        up = columns(a[f"ffn{n}_w_up"], P).reshape(L * C, P, W)
        return np.concatenate([gate, up], axis=2)

    w_in, w_out = a["mix_w_in"], a["mix_w_out"].reshape(L, KT, P, D)
    part = [w_in[:, :, i * GROUP:(i + 1) * GROUP] for i in range(7)]
    wa, wp, wb, wc, wh, wu, wv = part
    pv = np.concatenate([wp, wv], axis=2).reshape(L, 2, 4, P, 2 * GROUP).transpose(0, 1, 3, 2, 4)
    pv = pv.reshape(L, 2, P, 2 * W)
    ta, tb, tc, th, tu = [columns(w, P).reshape(L, CT, P, W) for w in (wa, wb, wc, wh, wu)]

    def pair(m, n):
        return np.concatenate([m, n], axis=2)

    mix_pairs = np.stack([
        pv[:, 0], pv[:, 1], pair(ta[:, 0], ta[:, 1]), pair(tc[:, 0], th[:, 0]), pair(tc[:, 1], th[:, 1]),
        pair(tu[:, 0], tu[:, 1]), pair(w_out[:, 0], w_out[:, 1]), pair(w_out[:, 2], w_out[:, 3])], axis=1)
    mix_singles = np.stack([tb[:, 0], tb[:, 1], w_out[:, 4], w_out[:, 5], w_out[:, 6], w_out[:, 7]], axis=1)
    conv = a["conv_w"].reshape(L, 3, CT, P).transpose(0, 3, 1, 2)
    small = np.concatenate([a["pool_scale"].reshape(L, 1, CT, P).transpose(0, 3, 1, 2), conv], axis=2)

    def by_parity(w):
        return w.reshape(L, CT, 2, *w.shape[2:])

    arrays = {
        "x": a["x"].reshape(SEQ, D),
        "ffn_pairs": np.stack([ffn_pairs(1), ffn_pairs(2)]),
        "ffn_singles": np.stack([a["ffn1_w_down"].reshape(L * C, P, D), a["ffn2_w_down"].reshape(L * C, P, D)]),
        "mix_pairs": mix_pairs.reshape(L * MIX_PAIRS, P, 2 * W),
        "mix_singles": mix_singles.reshape(L * MIX_SINGLES, P, W),
        "ln_params": np.stack([a[f"ln{s}_{w}"] for s in (1, 2, 3) for w in "gb"], axis=1),
        "v_params": np.stack([a["gmlp_ln_g"], a["gmlp_ln_b"]], axis=1),
        "gate_bias": by_parity(a["gmlp_b_s"]).transpose(0, 2, 1, 3),
        "pool_w": by_parity(a["pool_w"]).transpose(0, 2, 3, 1, 4),
        "small": small.reshape(L, P, 4 * CT),
        "spatial_w": a["gmlp_w_s"].transpose(0, 3, 1, 2),
        **constants(),
    }
    nc = bacc.Bacc("TRN2", target_bir_lowering=False, num_devices=1)
    sent, args = {}, []
    for name, v in arrays.items():
        v = np.ascontiguousarray(v, dtype=np.float32)
        sent[name + "_dram"] = v
        args.append(nc.dram_tensor(name + "_dram", v.shape, F32, kind="ExternalInput").ap())
    args.append(nc.dram_tensor("out_dram", (SEQ, D), F32, kind="ExternalOutput").ap())
    build(nc, *args)
    r = run(nc, [sent], core_ids=[0])
    return r.results[0]["out_dram"].reshape(1, SEQ, D)
```

```python
from contextlib import ExitStack

import numpy as np

import concourse.bass as bass
from concourse import mybir

ALU = mybir.AluOpType
ACT = mybir.ActivationFunctionType
F32 = mybir.dt.float32
F32R = mybir.dt.float32r

P = 128
LAYERS = 2
SEQ = 256
D = 1024
DFF = 2816
GROUP = 256
HEADS = 4
HEAD = GROUP // HEADS
CHUNK = 128
WINDOWS = (2, 4, 8, 16)
POOL_REACH = max(WINDOWS) // 2
ALPHA = (2 * LAYERS) ** 0.25
LN_EPS = 1e-5

TT = SEQ // P
KT = D // P
HALF = D // 2
CT = GROUP // P
CHUNKS = DFF // P
W = 1024

MIX_PAIRS = 8
MIX_SINGLES = 6
PAIRS = 2 * CHUNKS + MIX_PAIRS
SINGLES = 2 * CHUNKS + MIX_SINGLES
FFN_PAIR0 = (0, CHUNKS + MIX_PAIRS)
FFN_SINGLE0 = (0, CHUNKS + MIX_SINGLES)
MIX_PAIR0 = CHUNKS
MIX_SINGLE0 = CHUNKS
LAST_SINGLE = (CHUNKS - 1, CHUNKS + MIX_SINGLES - 1, SINGLES - 1)
STAGES = 3
LN_COUNTS = 6
MIX_COUNTS = 21


def build(nc, x, ffn_pairs, ffn_singles, mix_pairs, mix_singles, ln_params, v_params, gate_bias,
          pool_w, small, spatial_w, ident_c, dft_channels, dft_tokens, pool_matrix, out):
    with ExitStack() as ctx:
        def sb(name, shape, dt=F32):
            return ctx.enter_context(nc.sbuf_tensor(name, shape, dt))

        def sem(name):
            return ctx.enter_context(nc.semaphore(name))

        raw_pair = sb("raw_pair", [P, 2, 2 * W])
        raw_single = sb("raw_single", [P, 2, W])
        hi_pair = sb("hi_pair", [P, 2, 2, W], F32R)
        lo_pair = sb("lo_pair", [P, 2, 2, W], F32R)
        hi_single = sb("hi_single", [P, 2, W], F32R)
        lo_single = sb("lo_single", [P, 2, W], F32R)
        x_tok = sb("x_tok", [P, TT, D])
        xT_hi = sb("xT_hi", [P, KT, SEQ], F32R)
        xT_lo = sb("xT_lo", [P, KT, SEQ], F32R)
        res = sb("res", [P, D])
        res_hi = sb("res_hi", [P, TT, D], F32R)
        res_lo = sb("res_lo", [P, TT, D], F32R)
        silu_g = sb("silu_g", [P, 2, SEQ])
        hid = sb("hid", [P, 2, SEQ])
        hid_hi = sb("hid_hi", [P, 2, SEQ], F32R)
        hid_lo = sb("hid_lo", [P, 2, SEQ], F32R)
        centred = sb("centred", [P, 2, HALF])
        stats = sb("stats", [P, 2, 6])
        mean_var = sb("mean_var", [P, TT, 2])
        var_eps = sb("var_eps", [P, TT])
        std = sb("std", [P, TT])
        rstd = sb("rstd", [P, 1])
        ln = sb("ln", [P, 2 * STAGES, D])
        vln = sb("vln", [P, 2, GROUP])
        bias_s = sb("bias_s", [P, CT, CHUNK])
        pool_bd = sb("pool_bd", [P, CT, P])
        chan = sb("chan", [P, 4 * CT])
        ws = sb("ws", [P, HEADS, CHUNK])
        ident = sb("ident", [P, P])
        ident_r = sb("ident_r", [P, P], F32R)
        dft_ch = sb("dft_ch", [P, 2 * P])
        dft_tok = sb("dft_tok", [P, 2, TT, SEQ])
        pool_m = sb("pool_m", [P, HEADS, TT, SEQ])
        aT = sb("aT", [P, CT, SEQ])
        y1 = sb("y1", [P, TT, 2 * GROUP])
        p_tok = sb("p_tok", [P, TT, GROUP])
        pooled = aT
        v_mid = sb("v_mid", [P, GROUP])
        v_tok = sb("v_tok", [P, TT, GROUP])
        c_gate = sb("c_gate", [P, SEQ])
        z_pad = sb("z_pad", [P, SEQ + 2])
        conv = sb("conv", [P, SEQ])
        mixed = sb("mixed", [P, CT, SEQ])
        y_full = sb("y_full", [P, CT, SEQ])
        yT_hi = sb("yT_hi", [P, KT, SEQ], F32R)
        yT_lo = sb("yT_lo", [P, KT, SEQ], F32R)

        acc = ctx.enter_context(nc.psum_tensor("acc", [P, 2 * TT, HALF], F32))
        work = ctx.enter_context(nc.psum_tensor("work", [P, 4, HALF], F32))

        pair_landed = [[sem(f"pair_landed{i}{a}") for a in range(2)] for i in range(2)]
        single_landed = [sem(f"single_landed{i}") for i in range(2)]
        hi_pair_ready, hi_single_ready = sem("hi_pair_ready"), sem("hi_single_ready")
        lo_pair_ready, lo_single_ready = sem("lo_pair_ready"), sem("lo_single_ready")
        pair_used, single_used = sem("pair_used"), sem("single_used")
        x_landed = [sem(f"x_landed{t}") for t in range(TT)]
        x_ready = sem("x_ready")
        transposed = sem("transposed")
        xT_hi_ready, xT_lo_ready = sem("xT_hi_ready"), sem("xT_lo_ready")
        res_step, res_ready = sem("res_step"), sem("res_ready")
        silu_ready, hid_step, hid_ready = sem("silu_ready"), sem("hid_step"), sem("hid_ready")
        tok_done, tok_hid_ready = sem("tok_done"), sem("tok_hid_ready")
        hid_transposed, hidT_hi_ready = sem("hid_transposed"), sem("hidT_hi_ready")
        acc_done = sem("acc_done")
        ln_step, var_ready, std_ready = sem("ln_step"), sem("var_ready"), sem("std_ready")
        const_landed, ident_landed = sem("const_landed"), sem("ident_landed")
        ident_ready, bd_zeroed, pad_zeroed = sem("ident_ready"), sem("bd_zeroed"), sem("pad_zeroed")
        params_landed = sem("params_landed")
        mix_step = sem("mix_step")
        p_ready, aT_ready, y1_ready = sem("p_ready"), sem("aT_ready"), sem("y1_ready")
        v_var_ready, v_std_ready, v_ready = sem("v_var_ready"), sem("v_std_ready"), sem("v_ready")
        c_ready, z_ready = sem("c_ready"), sem("z_ready")
        dft1_done, pool_done, dft2_done = sem("dft1_done"), sem("pool_done"), sem("dft2_done")
        pooled_ready, pool_w_done, scaled_ready = sem("pooled_ready"), sem("pool_w_done"), sem("scaled_ready")
        spatial_done, mixed_ready = sem("spatial_done"), sem("mixed_ready")
        ya_hi_ready, ya_ready, yb_ready = sem("ya_hi_ready"), sem("ya_ready"), sem("yb_ready")
        yc_ready, yd_ready = sem("yc_ready"), sem("yd_ready")
        stored = sem("stored")
        dve_passed, pool_passed = sem("dve_passed"), sem("pool_passed")

        FREE_PAIR_TILES = 4
        FREE_SINGLES = 2
        PARAM_LOADS = 9
        CONST_LOADS = 3

        def pair_tiles(l, n, i=0):
            return (2 * PAIRS) * l + 2 * n + 4 * i

        def singles(l, n, i=0):
            return SINGLES * l + n + 2 * i

        def pair_loads(l, n, i=0):
            return (PAIRS // 2) * l + n // 2 + i

        def single_loads(l, n, i=0):
            return (SINGLES // 2) * l + n // 2 + i

        block = ctx.enter_context(nc.Block())

        @block.sync
        def _(sp):
            def load_pair(l, n, src, i=0):
                for a in range(2):
                    sp.wait_ge(lo_pair_ready, pair_tiles(l, n, i) - 3 + a + FREE_PAIR_TILES)
                    sp.dma_start(raw_pair[:, n % 2, a * W:(a + 1) * W], src[:, a * W:(a + 1) * W])\
                        .then_inc(pair_landed[n % 2][a], 16)

            def load_single(l, n, src, i=0):
                sp.wait_ge(lo_single_ready, singles(l, n, i) - 1 + FREE_SINGLES)
                sp.dma_start(raw_single[:, n % 2, :], src).then_inc(single_landed[n % 2], 16)

            def ffn_pair(l, f, j, i=0):
                load_pair(l, FFN_PAIR0[f] + j, ffn_pairs[f, (l * CHUNKS + j) + 2 * i], i)

            def ffn_single(l, f, j, i=0):
                load_single(l, FFN_SINGLE0[f] + j, ffn_singles[f, (l * CHUNKS + j) + 2 * i], i)

            def mix_pair(l, g):
                load_pair(l, MIX_PAIR0 + g, mix_pairs[l * MIX_PAIRS + g])

            def mix_single(l, g):
                load_single(l, MIX_SINGLE0 + g, mix_singles[l * MIX_SINGLES + g])

            sp.dma_start(x_tok[:, 0, :], x[0:P, :]).then_inc(x_landed[0], 16)
            with sp.Fori(0, LAYERS) as l:
                ffn_pair(l, 0, 0)
                ffn_pair(l, 0, 1)
                ffn_single(l, 0, 0)
                with sp.Fori(0, (CHUNKS - 2) // 2) as i:
                    for j in (0, 1):
                        ffn_pair(l, 0, j + 2, i)
                        ffn_single(l, 0, j + 1, i)
                mix_pair(l, 0)
                ffn_single(l, 0, CHUNKS - 1)
                mix_pair(l, 1)
                mix_single(l, 0)
                mix_single(l, 1)
                for g in (2, 3, 4, 5):
                    mix_pair(l, g)
                mix_single(l, 2)
                mix_pair(l, 6)
                mix_single(l, 3)
                mix_pair(l, 7)
                mix_single(l, 4)
                mix_single(l, 5)
                ffn_pair(l, 1, 0)
                ffn_pair(l, 1, 1)
                ffn_single(l, 1, 0)
                with sp.Fori(0, (CHUNKS - 2) // 2) as i:
                    for j in (0, 1):
                        ffn_pair(l, 1, j + 2, i)
                        ffn_single(l, 1, j + 1, i)
                ffn_single(l, 1, CHUNKS - 1)
            for t in range(TT):
                for h in range(2):
                    cols = slice(h * HALF, (h + 1) * HALF)
                    sp.wait_ge(x_ready, 2 * TT * (STAGES * LAYERS) + 2 * t + h + 1)
                    sp.dma_start(out[t * P:(t + 1) * P, cols], x_tok[:, t, cols]).then_inc(stored, 16)
            sp.wait_ge(stored, 16 * 2 * TT)

        @block.gpsimd
        def _(pool):
            nc.gpsimd.memset(pool_bd[:, :, :], 0.0).then_inc(bd_zeroed, 1)
            nc.gpsimd.memset(z_pad[:, :], 0.0).then_inc(pad_zeroed, 1)
            pool.wait_ge(x_landed[0], 16)
            pool.dma_start(x_tok[:, 1, :], x[P:2 * P, :]).then_inc(x_landed[1], 16)
            for t in range(TT):
                pool.wait_ge(x_landed[t], 16)
                nc.gpsimd.sem_inc(x_ready, 2)
            pool.wait_ge(pair_landed[1][1], 16)
            pool.wait_ge(bd_zeroed, 1)
            pool.dma_start(dft_ch[:, :], dft_channels).then_inc(const_landed, 16)
            pool.dma_start(dft_tok[:, :, :, :], dft_tokens).then_inc(const_landed, 16)
            pool.dma_start(pool_m[:, :, :, :], pool_matrix).then_inc(const_landed, 16)

            def residual(l, s):
                scale = ALPHA if s == 1 else 2 * ALPHA
                for t in range(TT):
                    n = TT * STAGES * l + TT * s + t
                    pool.wait_ge(x_ready, 2 * n + 2)
                    if t > 0:
                        pool.wait_ge(res_ready, n)
                    nc.gpsimd.sem_inc(pool_passed, 1)
                    nc.gpsimd.tensor_scalar(res[:, :], x_tok[:, t, :], scale, 0.0, ALU.mult, ALU.add)\
                        .then_inc(res_step, 1)
                    pool.wait_ge(res_step, 2 * n + 1)
                    nc.gpsimd.sem_inc(pool_passed, 1)
                    nc.gpsimd.tensor_scalar(res_hi[:, t, :], res[:, :], 1.0, 0.0, ALU.mult, ALU.add)\
                        .then_inc(res_step, 1)
                    pool.wait_ge(res_step, 2 * n + 2)
                    nc.gpsimd.tensor_tensor(res_lo[:, t, :], res[:, :], res_hi[:, t, :].bitcast(F32),
                                            ALU.subtract).then_inc(res_ready, 1)

            with pool.Fori(0, LAYERS) as l:
                residual(l, 0)
                pool.dma_start(ln[:, :, :], ln_params[l].partition_broadcast(P)).then_inc(params_landed, 16)
                pool.dma_start(vln[:, :, :], v_params[l].partition_broadcast(P)).then_inc(params_landed, 16)
                for hh in range(2):
                    at = slice(hh * HEAD, (hh + 1) * HEAD)
                    pool.dma_start(bias_s[at, :, :], gate_bias[l, hh].partition_broadcast(HEAD))\
                        .then_inc(params_landed, 16)
                    pool.dma_start(pool_bd[at, :, at], pool_w[l, hh]).then_inc(params_landed, 16)
                pool.dma_start(chan[:, :], small[l]).then_inc(params_landed, 16)
                pool.dma_start(ws[:, 0:2, :], spatial_w[l, :, 0:2, :]).then_inc(params_landed, 16)
                pool.dma_start(ws[:, 2:4, :], spatial_w[l, :, 2:4, :]).then_inc(params_landed, 16)
                residual(l, 1)
                residual(l, 2)

        @block.scalar
        def _(act):
            def copy(dst, src):
                return nc.scalar.activation(dst, src, ACT.Copy)

            def hi_of_pair(l, n, i=0):
                for a in range(2):
                    act.wait_ge(pair_landed[n % 2][a], 16 * pair_loads(l, n, i) + 16)
                    act.wait_ge(pair_used, pair_tiles(l, n, i) - 3 + a + FREE_PAIR_TILES)
                    copy(hi_pair[:, n % 2, a, :], raw_pair[:, n % 2, a * W:(a + 1) * W])\
                        .then_inc(hi_pair_ready, 1)

            def hi_of_single(l, n, i=0):
                act.wait_ge(single_landed[n % 2], 16 * single_loads(l, n, i) + 16)
                act.wait_ge(single_used, singles(l, n, i) - 1 + FREE_SINGLES)
                copy(hi_single[:, n % 2, :], raw_single[:, n % 2, :]).then_inc(hi_single_ready, 1)

            def spread(l, s, t):
                for h in range(2):
                    n = 2 * TT * STAGES * l + 2 * TT * s + 2 * t + h
                    act.wait_ge(transposed, n + 1)
                    copy(xT_hi[:, 4 * h:4 * h + 4, t * P:(t + 1) * P],
                         acc[:, 2 * t + h, :].rearrange("p (k n) -> p k n", k=4)).then_inc(xT_hi_ready, 1)

            def deviation(l, s, t):
                act.wait_ge(var_ready, TT * STAGES * l + TT * s + t + 1)
                nc.scalar.activation(std[:, t:t + 1], var_eps[:, t:t + 1], ACT.Sqrt).then_inc(std_ready, 1)

            def between_stages(l, s):
                deviation(l, s, 0)
                spread(l, s + 1, 0)
                deviation(l, s, 1)
                spread(l, s + 1, 1)

            def silu(l, f, j, i=0):
                act.wait_ge(pair_used, pair_tiles(l, FFN_PAIR0[f] + j, i) + 1 + FREE_PAIR_TILES)
                nc.scalar.activation(silu_g[:, j % 2, :], work[:, 2 * (j % 2), 0:SEQ], ACT.Silu)\
                    .then_inc(silu_ready, 1)

            def silu_tok(l, f, j, t):
                if t == 0:
                    act.wait_ge(tok_done, 4 * l + 2 * f + j + 1)
                else:
                    act.wait_ge(pair_used, pair_tiles(l, FFN_PAIR0[f] + j) + 2 + FREE_PAIR_TILES)
                nc.scalar.activation(silu_g[:, j, t * P:(t + 1) * P], work[:, 2 * j + t, 0:P], ACT.Silu)\
                    .then_inc(silu_ready, 1)

            def hidT_hi(l, f, j):
                act.wait_ge(hid_transposed, 4 * l + 2 * f + j + 1)
                copy(hid_hi[:, j, :], work[:, 2 * j, 0:SEQ]).then_inc(hidT_hi_ready, 1)

            def ffn(l, f, after_20, after_21):
                def step(j, i=0):
                    silu(l, f, j, i)
                    hi_of_pair(l, FFN_PAIR0[f] + j + 2, i)
                    hi_of_single(l, FFN_SINGLE0[f] + j + 1, i)

                silu_tok(l, f, 0, 0)
                silu_tok(l, f, 1, 0)
                hi_of_single(l, FFN_SINGLE0[f] + 1)
                silu_tok(l, f, 0, 1)
                hi_of_pair(l, FFN_PAIR0[f] + 2)
                silu_tok(l, f, 1, 1)
                hidT_hi(l, f, 0)
                hi_of_pair(l, FFN_PAIR0[f] + 3)
                hidT_hi(l, f, 1)
                hi_of_single(l, FFN_SINGLE0[f] + 2)
                with act.Fori(0, (CHUNKS - 4) // 2) as i:
                    step(2, i)
                    step(3, i)
                silu(l, f, 20)
                after_20()
                silu(l, f, 21)
                after_21()

            act.dma_start(ident[:, :], ident_c).then_inc(ident_landed, 16)
            act.wait_ge(ident_landed, 16)
            copy(ident_r[:, :], ident[:, :]).then_inc(ident_ready, 1)
            with act.Fori(0, LAYERS) as l:
                spread(l, 0, 0)
                hi_of_pair(l, 0)
                hi_of_pair(l, 1)
                spread(l, 0, 1)
                hi_of_single(l, 0)

                def mix_pair(g):
                    hi_of_pair(l, MIX_PAIR0 + g)

                def mix_single(g):
                    hi_of_single(l, MIX_SINGLE0 + g)

                def into_mixer_20():
                    mix_pair(0)
                    hi_of_single(l, CHUNKS - 1)

                def into_mixer_21():
                    mix_pair(1)

                def to_end_20():
                    hi_of_single(l, FFN_SINGLE0[1] + CHUNKS - 1)

                ffn(l, 0, into_mixer_20, into_mixer_21)
                between_stages(l, 0)

                mix_single(0)
                mix_single(1)
                mix_pair(2)
                mix_pair(3)
                for t in range(TT):
                    act.wait_ge(pair_used, pair_tiles(l, MIX_PAIR0 + 2) + FREE_PAIR_TILES)
                    copy(p_tok[:, t, :], acc[:, t, 0:GROUP]).then_inc(p_ready, 1)
                for t in range(TT):
                    act.wait_ge(v_var_ready, TT * l + t + 1)
                    nc.scalar.activation(std[:, t:t + 1], var_eps[:, t:t + 1], ACT.Sqrt)\
                        .then_inc(v_std_ready, 1)
                act.wait_ge(pair_used, pair_tiles(l, MIX_PAIR0 + 3) + FREE_PAIR_TILES)
                copy(aT[:, :, :], work[:, 0, :].rearrange("p (c n) -> p c n", c=CT)).then_inc(aT_ready, 1)
                mix_pair(4)
                act.wait_ge(pair_used, pair_tiles(l, MIX_PAIR0 + 4) + FREE_PAIR_TILES)
                copy(c_gate[:, :], work[:, 1, 0:SEQ]).then_inc(c_ready, 1)
                mix_pair(5)
                for t in range(TT):
                    act.wait_ge(dft1_done, TT * l + t + 1)
                    copy(y1[:, t, :], acc[:, TT + t, :]).then_inc(y1_ready, 1)
                mix_single(2)
                act.wait_ge(pair_used, pair_tiles(l, MIX_PAIR0 + 5) + FREE_PAIR_TILES)
                act.wait_ge(z_ready, CT * l + 1)
                copy(c_gate[:, :], work[:, 3, 0:SEQ]).then_inc(c_ready, 1)
                mix_pair(6)
                act.wait_ge(pool_done, l + 1)
                copy(pooled[:, :, :], work[:, 0, :].rearrange("p (c n) -> p c n", c=CT))\
                    .then_inc(pooled_ready, 1)
                mix_single(3)
                act.wait_ge(dft2_done, l + 1)
                copy(yT_hi[:, 0:2, :], acc[:, 1, :].rearrange("p (c n) -> p c n", c=CT))\
                    .then_inc(ya_hi_ready, 1)
                mix_pair(7)
                act.wait_ge(pool_w_done, l + 1)
                act.wait_ge(yc_ready, CT * l + CT)
                for c in range(CT):
                    nc.scalar.activation(y_full[:, c, :], work[:, 3, c * SEQ:(c + 1) * SEQ], ACT.Copy,
                                         scale=chan[:, c:c + 1]).then_inc(scaled_ready, 1)
                mix_single(4)
                mix_single(5)
                hi_of_pair(l, FFN_PAIR0[1])
                hi_of_pair(l, FFN_PAIR0[1] + 1)
                between_stages(l, 1)
                hi_of_single(l, FFN_SINGLE0[1])

                ffn(l, 1, to_end_20, lambda: None)
                for t in range(TT):
                    deviation(l, 2, t)

        @block.vector
        def _(dve):
            def lo_of_pair(l, n, i=0, tiles=(0, 1)):
                for a in tiles:
                    dve.wait_ge(hi_pair_ready, pair_tiles(l, n, i) + a + 1)
                    nc.vector.tensor_tensor(lo_pair[:, n % 2, a, :], raw_pair[:, n % 2, a * W:(a + 1) * W],
                                            hi_pair[:, n % 2, a, :].bitcast(F32), ALU.subtract)\
                        .then_inc(lo_pair_ready, 1)

            def lo_of_single(l, n, i=0):
                dve.wait_ge(hi_single_ready, singles(l, n, i) + 1)
                nc.vector.tensor_tensor(lo_single[:, n % 2, :], raw_single[:, n % 2, :],
                                        hi_single[:, n % 2, :].bitcast(F32), ALU.subtract)\
                    .then_inc(lo_single_ready, 1)

            def spread(l, s, t, halves=(0, 1)):
                for h in halves:
                    dve.wait_ge(xT_hi_ready, 2 * TT * STAGES * l + 2 * TT * s + 2 * t + h + 1)
                    at = (slice(None), slice(4 * h, 4 * h + 4), slice(t * P, (t + 1) * P))
                    nc.vector.tensor_tensor(xT_lo[at],
                                            acc[:, 2 * t + h, :].rearrange("p (k n) -> p k n", k=4),
                                            xT_hi[at].bitcast(F32), ALU.subtract).then_inc(xT_lo_ready, 1)

            def norm_stats(l, s, t, between=lambda: None):
                step = LN_COUNTS * (TT * STAGES * l + TT * s + t)
                if t == 0:
                    dve.wait_ge(acc_done, STAGES * l + s + 1)
                else:
                    dve.wait_ge(single_used, singles(l, LAST_SINGLE[s]) + 1 + FREE_SINGLES)
                nc.vector.bn_stats(stats[:, 0, :], acc[:, 2 * t, :]).then_inc(ln_step, 1)
                between()
                nc.vector.bn_stats(stats[:, 1, :], acc[:, 2 * t + 1, :]).then_inc(ln_step, 1)
                dve.wait_ge(ln_step, step + 2)
                nc.vector.sem_inc(dve_passed, 1)
                nc.vector.bn_aggr(mean_var[:, t, :], stats[:, :, :].rearrange("p a b -> p (a b)"))\
                    .then_inc(ln_step, 1)
                dve.wait_ge(ln_step, step + 3)
                nc.vector.tensor_scalar_add(var_eps[:, t:t + 1], mean_var[:, t, 1:2],
                                            LN_EPS if s == 1 else 4 * LN_EPS).then_inc(var_ready, 1)

            def norm_apply(l, s, t):
                n = TT * STAGES * l + TT * s + t
                step = LN_COUNTS * n
                if s == 0 and t == 0:
                    dve.wait_ge(params_landed, 16 * PARAM_LOADS * (l + 1))
                for h in range(2):
                    cols = slice(h * HALF, (h + 1) * HALF)
                    nc.vector.scalar_tensor_tensor(centred[:, h, :], acc[:, 2 * t + h, :], mean_var[:, t, 0:1],
                                                   ln[:, 2 * s, cols], ALU.subtract, ALU.mult)\
                        .then_inc(ln_step, 1)
                    if h == 0:
                        dve.wait_ge(std_ready, n + 1)
                        nc.vector.reciprocal(rstd[:, :], std[:, t:t + 1]).then_inc(ln_step, 1)
                    dve.wait_ge(ln_step, step + 5 + h)
                    nc.vector.scalar_tensor_tensor(x_tok[:, t, cols], centred[:, h, :], rstd[:, :],
                                                   ln[:, 2 * s + 1, cols], ALU.mult, ALU.add)\
                        .then_inc(x_ready, 1)

            def between_stages(l, s):
                norm_stats(l, s, 0)
                norm_apply(l, s, 0)
                norm_stats(l, s, 1, between=lambda: spread(l, s + 1, 0, halves=(0,)))
                spread(l, s + 1, 0, halves=(1,))
                norm_apply(l, s, 1)
                spread(l, s + 1, 1)

            def hidden_tok(l, f, j, t):
                dve.wait_ge(silu_ready, (CHUNKS + 2) * (2 * l + f) + 2 * t + j + 1)
                toks = slice(t * P, (t + 1) * P)
                nc.vector.tensor_tensor(hid[:, j, toks], silu_g[:, j, toks], work[:, 2 * j + t, P:2 * P],
                                        ALU.mult).then_inc(tok_hid_ready, 1)

            def hidT_lo(l, f, j):
                dve.wait_ge(hidT_hi_ready, 4 * l + 2 * f + j + 1)
                nc.vector.tensor_tensor(hid_lo[:, j, :], work[:, 2 * j, 0:SEQ], hid_hi[:, j, :].bitcast(F32),
                                        ALU.subtract).then_inc(hid_ready, 1)

            def hidden(l, f, j, i=0):
                n = (CHUNKS - 2) * (2 * l + f) + j - 2 + 2 * i
                dve.wait_ge(pair_used, pair_tiles(l, FFN_PAIR0[f] + j, i) + 2 + FREE_PAIR_TILES)
                dve.wait_ge(silu_ready, (CHUNKS + 2) * (2 * l + f) + j + 2 * i + 3)
                b = j % 2
                up = work[:, 2 * b + 1, 0:SEQ]
                nc.vector.tensor_tensor(hid[:, b, :], silu_g[:, b, :], up, ALU.mult).then_inc(hid_step, 1)
                dve.wait_ge(hid_step, 2 * n + 1)
                nc.vector.tensor_copy(hid_hi[:, b, :], hid[:, b, :]).then_inc(hid_step, 1)
                dve.wait_ge(hid_step, 2 * n + 2)
                nc.vector.tensor_tensor(hid_lo[:, b, :], hid[:, b, :], hid_hi[:, b, :].bitcast(F32),
                                        ALU.subtract).then_inc(hid_ready, 1)

            def ffn(l, f, after_20, before_21, after_21):
                def step(j, i=0):
                    hidden(l, f, j, i)
                    lo_of_pair(l, FFN_PAIR0[f] + j + 2, i)
                    lo_of_single(l, FFN_SINGLE0[f] + j + 1, i)

                hidden_tok(l, f, 0, 0)
                hidden_tok(l, f, 1, 0)
                lo_of_single(l, FFN_SINGLE0[f] + 1)
                hidden_tok(l, f, 0, 1)
                lo_of_pair(l, FFN_PAIR0[f] + 2)
                hidden_tok(l, f, 1, 1)
                hidT_lo(l, f, 0)
                lo_of_pair(l, FFN_PAIR0[f] + 3)
                hidT_lo(l, f, 1)
                lo_of_single(l, FFN_SINGLE0[f] + 2)
                with dve.Fori(0, (CHUNKS - 4) // 2) as i:
                    step(2, i)
                    step(3, i)
                hidden(l, f, 20)
                after_20()
                before_21()
                hidden(l, f, 21)
                after_21()

            nc.vector.sem_inc(lo_pair_ready, FREE_PAIR_TILES)
            nc.vector.sem_inc(lo_single_ready, FREE_SINGLES)
            dve.wait_ge(pad_zeroed, 1)

            with dve.Fori(0, LAYERS) as l:
                spread(l, 0, 0)
                lo_of_pair(l, 0)
                lo_of_pair(l, 1)
                spread(l, 0, 1)
                lo_of_single(l, 0)

                def mix_pair(g):
                    lo_of_pair(l, MIX_PAIR0 + g)

                def mix_single(g):
                    lo_of_single(l, MIX_SINGLE0 + g)

                def into_mixer_20():
                    mix_pair(0)
                    lo_of_single(l, CHUNKS - 1)

                def before_21():
                    lo_of_pair(l, MIX_PAIR0 + 1, tiles=(0,))

                def into_mixer_21():
                    lo_of_pair(l, MIX_PAIR0 + 1, tiles=(1,))

                def to_end_20():
                    lo_of_single(l, FFN_SINGLE0[1] + CHUNKS - 1)

                ffn(l, 0, into_mixer_20, before_21, into_mixer_21)
                between_stages(l, 0)

                count = [0]

                def chain(ins):
                    count[0] += 1
                    ins.then_inc(mix_step, 1)
                    dve.wait_ge(mix_step, MIX_COUNTS * l + count[0])

                mix_single(0)
                mix_single(1)
                mix_pair(2)
                mix_pair(3)
                dve.wait_ge(pair_used, pair_tiles(l, MIX_PAIR0 + 2) + FREE_PAIR_TILES)
                for t in range(TT):
                    dve.wait_ge(p_ready, TT * l + t + 1)
                    v = acc[:, t, GROUP:2 * GROUP]
                    chain(nc.vector.bn_stats(stats[:, 0, :], v))
                    nc.vector.sem_inc(dve_passed, 1)
                    chain(nc.vector.bn_aggr(mean_var[:, t, :], stats[:, 0, :]))
                    nc.vector.tensor_scalar_add(var_eps[:, t:t + 1], mean_var[:, t, 1:2], LN_EPS)\
                        .then_inc(v_var_ready, 1)
                    chain(nc.vector.scalar_tensor_tensor(v_mid[:, :], v, mean_var[:, t, 0:1], vln[:, 0, :],
                                                         ALU.subtract, ALU.mult))
                    dve.wait_ge(v_std_ready, TT * l + t + 1)
                    chain(nc.vector.reciprocal(rstd[:, :], std[:, t:t + 1]))
                    nc.vector.scalar_tensor_tensor(v_tok[:, t, :], v_mid[:, :], rstd[:, :], vln[:, 1, :],
                                                   ALU.mult, ALU.add).then_inc(v_ready, 1)
                mix_pair(4)

                def conv_group(c, h_at, b_at):
                    dve.wait_ge(c_ready, CT * l + c + 1)
                    nc.vector.tensor_tensor(z_pad[:, 1:SEQ + 1], c_gate[:, :], h_at, ALU.mult).then_inc(z_ready, 1)
                    dve.wait_ge(z_ready, CT * l + c + 1)

                    def w(k):
                        return chan[:, CT * (k + 1) + c:CT * (k + 1) + c + 1]

                    chain(nc.vector.tensor_scalar(conv[:, :], z_pad[:, 0:SEQ], w(0), None, ALU.mult))
                    for k in (1, 2):
                        chain(nc.vector.scalar_tensor_tensor(conv[:, :], z_pad[:, k:k + SEQ], w(k), conv[:, :],
                                                             ALU.mult, ALU.add))
                    dve.wait_ge(single_used, singles(l, MIX_SINGLE0 + c) + 1 + FREE_SINGLES)
                    chain(nc.vector.tensor_tensor(y_full[:, c, :], conv[:, :], b_at, ALU.mult))
                    chain(nc.vector.tensor_copy(yT_hi[:, 4 + c, :], y_full[:, c, :]))
                    nc.vector.tensor_tensor(yT_lo[:, 4 + c, :], y_full[:, c, :], yT_hi[:, 4 + c, :].bitcast(F32),
                                            ALU.subtract).then_inc(yc_ready, 1)

                conv_group(0, work[:, 1, SEQ:2 * SEQ], work[:, 2, 0:SEQ])
                mix_pair(5)
                mix_single(2)
                conv_group(1, work[:, 3, SEQ:2 * SEQ], work[:, 2, SEQ:2 * SEQ])
                mix_pair(6)
                dve.wait_ge(spatial_done, l + 1)
                for c in range(CT):
                    last = nc.vector.tensor_tensor(
                        mixed[:, c, :].rearrange("p (t q) -> p t q", t=TT),
                        acc[:, 0, c * SEQ:(c + 1) * SEQ].rearrange("p (t q) -> p t q", t=TT),
                        bias_s[:, c, :].unsqueeze(1).to_broadcast([P, TT, CHUNK]), ALU.add)
                    last.then_inc(mixed_ready, 1)
                mix_single(3)
                dve.wait_ge(ya_hi_ready, l + 1)
                nc.vector.tensor_tensor(yT_lo[:, 0:2, :], acc[:, 1, :].rearrange("p (c n) -> p c n", c=CT),
                                        yT_hi[:, 0:2, :].bitcast(F32), ALU.subtract).then_inc(ya_ready, 1)
                mix_pair(7)
                dve.wait_ge(scaled_ready, CT * (l + 1))
                chain(nc.vector.tensor_copy(yT_hi[:, 2:4, :], y_full[:, :, :]))
                nc.vector.tensor_tensor(yT_lo[:, 2:4, :], y_full[:, :, :], yT_hi[:, 2:4, :].bitcast(F32),
                                        ALU.subtract).then_inc(yb_ready, 1)
                mix_single(4)
                dve.wait_ge(pair_used, pair_tiles(l, MIX_PAIR0 + 6) + FREE_PAIR_TILES)
                dve.wait_ge(mixed_ready, CT * (l + 1))
                dve.wait_ge(yb_ready, l + 1)
                chain(nc.vector.tensor_tensor(y_full[:, :, :], mixed[:, :, :],
                                              work[:, 1, :].rearrange("p (c n) -> p c n", c=CT), ALU.mult))
                chain(nc.vector.tensor_copy(yT_hi[:, 6:8, :], y_full[:, :, :]))
                nc.vector.tensor_tensor(yT_lo[:, 6:8, :], y_full[:, :, :], yT_hi[:, 6:8, :].bitcast(F32),
                                        ALU.subtract).then_inc(yd_ready, 1)
                assert count[0] == MIX_COUNTS, count
                mix_single(5)
                lo_of_pair(l, FFN_PAIR0[1])
                lo_of_pair(l, FFN_PAIR0[1] + 1)
                between_stages(l, 1)
                lo_of_single(l, FFN_SINGLE0[1])

                ffn(l, 1, to_end_20, lambda: None, lambda: None)
                for t in range(TT):
                    norm_stats(l, 2, t)
                    norm_apply(l, 2, t)

        @block.tensor
        def _(pe):
            def exact(dst, w_hi, w_lo, m_hi, m_lo, first, last):
                nc.tensor.matmul(dst, w_hi, m_hi, start=first, stop=False)
                nc.tensor.matmul(dst, w_hi, m_lo, start=False, stop=False)
                return nc.tensor.matmul(dst, w_lo, m_hi, start=False, stop=last)

            def transpose_x(l, s, t):
                for h in range(2):
                    n = 2 * TT * STAGES * l + 2 * TT * s + 2 * t + h
                    pe.wait_ge(x_ready, n + 1)
                    for k in range(4):
                        col = h * HALF + k * P
                        last = nc.tensor.transpose(acc[:, 2 * t + h, k * P:(k + 1) * P],
                                                   x_tok[:, t, col:col + P], ident[:, :])
                    last.then_inc(transposed, 1)

            def spread_done(l, s, t, k):
                if k % 4 == 0:
                    pe.wait_ge(xT_lo_ready, 2 * TT * STAGES * l + 2 * TT * s + 2 * t + k // 4 + 1)

            def residual(l, s):
                for t in range(TT):
                    pe.wait_ge(res_ready, TT * STAGES * l + TT * s + t + 1)
                    for h in range(2):
                        cols = slice(h * HALF, (h + 1) * HALF)
                        nc.tensor.matmul(acc[:, 2 * t + h, :], ident_r[:, :], res_hi[:, t, cols],
                                         start=True, stop=False)
                        nc.tensor.matmul(acc[:, 2 * t + h, :], ident_r[:, :], res_lo[:, t, cols],
                                         start=False, stop=False)

            def channels_major(l, n, a, dst, i=0):
                pe.wait_ge(lo_pair_ready, pair_tiles(l, n, i) + a + 1 + FREE_PAIR_TILES)
                for k in range(KT):
                    at = slice(k * P, (k + 1) * P)
                    last = exact(dst, hi_pair[:, n % 2, a, at], lo_pair[:, n % 2, a, at],
                                 xT_hi[:, k, :], xT_lo[:, k, :], k == 0, k == KT - 1)
                last.then_inc(pair_used, 1)

            def gate_up(l, f, j, i=0):
                for a in range(2):
                    channels_major(l, FFN_PAIR0[f] + j, a, work[:, 2 * (j % 2) + a, 0:SEQ], i)

            def gate_up_tok(l, f, j, t, between=None):
                n = FFN_PAIR0[f] + j
                pe.wait_ge(lo_pair_ready, pair_tiles(l, n) + 2 + FREE_PAIR_TILES)
                toks = slice(t * P, (t + 1) * P)
                for k in range(KT):
                    if k == KT // 2 and between is not None:
                        between()
                    if j == 0:
                        spread_done(l, 2 * f, t, k)
                    at = slice(k * P, (k + 1) * P)
                    last = exact(work[:, 2 * j + t, 0:2 * P], xT_hi[:, k, toks], xT_lo[:, k, toks],
                                 hi_pair[:, n % 2, :, at], lo_pair[:, n % 2, :, at], k == 0, k == KT - 1)
                if t == 0:
                    last.then_inc(tok_done, 1)
                else:
                    last.then_inc(pair_used, 2)

            def transpose_hidden(l, f, j):
                for t in range(TT):
                    pe.wait_ge(tok_hid_ready, 8 * l + 4 * f + 2 * t + j + 1)
                for t in range(TT):
                    toks = slice(t * P, (t + 1) * P)
                    last = nc.tensor.transpose(work[:, 2 * j, toks], hid[:, j, toks], ident[:, :])
                last.then_inc(hid_transposed, 1)

            def first_chunks(l, f):
                s = 2 * f
                transpose_x(l, s, 0)
                gate_up_tok(l, f, 0, 0)
                gate_up_tok(l, f, 1, 0, between=lambda: transpose_x(l, s, 1))
                gate_up_tok(l, f, 0, 1)
                gate_up_tok(l, f, 1, 1)
                transpose_hidden(l, f, 0)
                residual(l, s)
                transpose_hidden(l, f, 1)

            def down(l, f, j, i=0):
                n = FFN_SINGLE0[f] + j
                pe.wait_ge(lo_single_ready, singles(l, n, i) + 1 + FREE_SINGLES)
                pe.wait_ge(hid_ready, 2 * CHUNKS * l + CHUNKS * f + j + 2 * i + 1)
                for t in range(TT):
                    last = to_output(t, hid_hi[:, j % 2, :], hid_lo[:, j % 2, :], hi_single[:, n % 2, :],
                                     lo_single[:, n % 2, :], False)
                last.then_inc(single_used, 1)

            def last_downs(l, f):
                for t in range(TT):
                    for j in (CHUNKS - 2, CHUNKS - 1):
                        n = FFN_SINGLE0[f] + j
                        if t == 0:
                            pe.wait_ge(lo_single_ready, singles(l, n) + 1 + FREE_SINGLES)
                            pe.wait_ge(hid_ready, 2 * CHUNKS * l + CHUNKS * f + j + 1)
                        last = to_output(t, hid_hi[:, j % 2, :], hid_lo[:, j % 2, :], hi_single[:, n % 2, :],
                                         lo_single[:, n % 2, :], j == CHUNKS - 1)
                        if t == TT - 1:
                            last.then_inc(single_used, 1)
                    if t == 0:
                        last.then_inc(acc_done, 1)

            def to_output(t, y_hi, y_lo, w_hi, w_lo, final):
                toks = slice(t * P, (t + 1) * P)
                for h in range(2):
                    cols = slice(h * HALF, (h + 1) * HALF)
                    last = exact(acc[:, 2 * t + h, :], y_hi[:, toks], y_lo[:, toks], w_hi[:, cols],
                                 w_lo[:, cols], False, final)
                return last

            def ffn(l, f):
                first_chunks(l, f)
                down(l, f, 0)
                with pe.Fori(0, (CHUNKS - 4) // 2) as i:
                    for j in (2, 3):
                        gate_up(l, f, j, i)
                        down(l, f, j - 1, i)
                gate_up(l, f, CHUNKS - 2)
                down(l, f, CHUNKS - 3)
                gate_up(l, f, CHUNKS - 1)
                last_downs(l, f)

            nc.tensor.sem_inc(pair_used, FREE_PAIR_TILES)
            nc.tensor.sem_inc(single_used, FREE_SINGLES)
            pe.wait_ge(ident_landed, 16)
            pe.wait_ge(ident_ready, 1)
            with pe.Fori(0, LAYERS) as l:
                ffn(l, 0)

                transpose_x(l, 1, 0)
                for t in range(TT):
                    toks = slice(t * P, (t + 1) * P)
                    for g, a in ((0, 0), (0, 1), (1, 0), (1, 1)):
                        if t == 0 and (g, a) == (1, 1):
                            transpose_x(l, 1, 1)
                        n = MIX_PAIR0 + g
                        pe.wait_ge(lo_pair_ready, pair_tiles(l, n) + a + 1 + FREE_PAIR_TILES)
                        for kk in range(2):
                            k = 4 * g + 2 * a + kk
                            spread_done(l, 1, t, k)
                            at = slice(kk * HALF, (kk + 1) * HALF)
                            last = exact(acc[:, t, :], xT_hi[:, k, toks], xT_lo[:, k, toks],
                                         hi_pair[:, n % 2, a, at], lo_pair[:, n % 2, a, at],
                                         k == 0, k == KT - 1)
                        if t == TT - 1:
                            last.then_inc(pair_used, 1)
                for c in range(CT):
                    channels_major(l, MIX_PAIR0 + 2, c, work[:, 0, c * SEQ:(c + 1) * SEQ])

                def gate_b(c):
                    n = MIX_SINGLE0 + c
                    pe.wait_ge(lo_single_ready, singles(l, n) + 1 + FREE_SINGLES)
                    for k in range(KT):
                        at = slice(k * P, (k + 1) * P)
                        last = exact(work[:, 2, c * SEQ:(c + 1) * SEQ], hi_single[:, n % 2, at],
                                     lo_single[:, n % 2, at], xT_hi[:, k, :], xT_lo[:, k, :],
                                     k == 0, k == KT - 1)
                    last.then_inc(single_used, 1)

                channels_major(l, MIX_PAIR0 + 3, 0, work[:, 1, 0:SEQ])
                channels_major(l, MIX_PAIR0 + 3, 1, work[:, 1, SEQ:2 * SEQ])
                gate_b(0)
                pe.wait_ge(const_landed, 16 * CONST_LOADS)
                pe.wait_ge(aT_ready, l + 1)
                for t in range(TT):
                    for c in range(CT):
                        last = nc.tensor.matmul(acc[:, TT + t, c * 2 * P:(c + 1) * 2 * P],
                                                aT[:, c, t * P:(t + 1) * P], dft_ch[:, :], start=True, stop=True)
                    last.then_inc(dft1_done, 1)
                channels_major(l, MIX_PAIR0 + 4, 0, work[:, 3, 0:SEQ])
                channels_major(l, MIX_PAIR0 + 4, 1, work[:, 3, SEQ:2 * SEQ])
                pe.wait_ge(yc_ready, CT * l + 1)
                gate_b(1)
                pe.wait_ge(p_ready, TT * (l + 1))
                for g in range(HEADS):
                    dst = work[(g % 2) * HEAD:(g % 2 + 1) * HEAD, 0, (g // 2) * SEQ:(g // 2 + 1) * SEQ]
                    for t in range(TT):
                        to = slice(0, P + POOL_REACH) if t == 0 else slice(P - POOL_REACH, SEQ)
                        last = nc.tensor.matmul(dst[:, to], p_tok[:, t, g * HEAD:(g + 1) * HEAD],
                                                pool_m[:, g, t, to], start=(t == 0), stop=(t == TT - 1),
                                                skip_group_check=True)
                last.then_inc(pool_done, 1)
                pe.wait_ge(v_ready, TT * (l + 1))
                pe.wait_ge(params_landed, 16 * PARAM_LOADS * (l + 1))
                for g in range(HEADS):
                    for t in range(TT):
                        col = (g // 2) * SEQ + t * P
                        dst = acc[(g % 2) * HEAD:(g % 2 + 1) * HEAD, 0, col:col + P]
                        last = nc.tensor.matmul(dst, v_tok[:, t, g * HEAD:(g + 1) * HEAD], ws[:, g, :],
                                                start=True, stop=True)
                last.then_inc(spatial_done, 1)
                pe.wait_ge(y1_ready, TT * (l + 1))
                for c in range(CT):
                    for t in range(TT):
                        for part in range(2):
                            col = c * 2 * P + part * P
                            last = nc.tensor.matmul(acc[:, 1, c * SEQ:(c + 1) * SEQ], y1[:, t, col:col + P],
                                                    dft_tok[:, part, t, :], start=(t == 0 and part == 0),
                                                    stop=(t == TT - 1 and part == 1))
                last.then_inc(dft2_done, 1)
                pe.wait_ge(z_ready, CT * l + 1)
                for c in range(CT):
                    channels_major(l, MIX_PAIR0 + 5, c, work[:, 1, c * SEQ:(c + 1) * SEQ])
                pe.wait_ge(pooled_ready, l + 1)
                pe.wait_ge(z_ready, CT * (l + 1))
                for c in range(CT):
                    last = nc.tensor.matmul(work[:, 3, c * SEQ:(c + 1) * SEQ], pool_bd[:, c, :],
                                            pooled[:, c, :], start=True, stop=True)
                last.then_inc(pool_w_done, 1)
                pe.wait_ge(mixed_ready, CT * (l + 1))
                pe.wait_ge(ya_ready, l + 1)
                residual(l, 1)

                def out_pair(g, k0):
                    n = MIX_PAIR0 + g
                    for a in range(2):
                        pe.wait_ge(lo_pair_ready, pair_tiles(l, n) + a + 1 + FREE_PAIR_TILES)
                        for t in range(TT):
                            last = to_output(t, yT_hi[:, k0 + a, :], yT_lo[:, k0 + a, :],
                                             hi_pair[:, n % 2, a, :], lo_pair[:, n % 2, a, :], False)
                        last.then_inc(pair_used, 1)

                def out_single(g, k, t, final=False):
                    n = MIX_SINGLE0 + g
                    pe.wait_ge(lo_single_ready, singles(l, n) + 1 + FREE_SINGLES)
                    last = to_output(t, yT_hi[:, k, :], yT_lo[:, k, :], hi_single[:, n % 2, :],
                                     lo_single[:, n % 2, :], final)
                    if t == TT - 1:
                        last.then_inc(single_used, 1)
                    return last

                out_pair(6, 0)
                pe.wait_ge(yc_ready, CT * (l + 1))
                for g, k in ((2, 4), (3, 5)):
                    for t in range(TT):
                        out_single(g, k, t)
                pe.wait_ge(yb_ready, l + 1)
                out_pair(7, 2)
                pe.wait_ge(yd_ready, l + 1)
                out_single(4, 6, 0)
                out_single(5, 7, 0, final=True).then_inc(acc_done, 1)
                out_single(4, 6, 1)
                out_single(5, 7, 1, final=True)

                ffn(l, 1)


def constants():
    n = np.arange(HEAD)
    ang = 2 * np.pi * np.outer(n, n) / HEAD
    ch = np.zeros((P, 2, 2, HEAD))
    for hh in range(2):
        ch[hh * HEAD:(hh + 1) * HEAD, 0, hh] = np.cos(ang)
        ch[hh * HEAD:(hh + 1) * HEAD, 1, hh] = np.sin(ang)
    ch = ch.reshape(P, 2 * P) / np.sqrt(HEAD)
    n = np.arange(SEQ)
    ang = 2 * np.pi * (np.outer(n, n) % SEQ) / SEQ
    tok = np.stack([np.cos(ang), -np.sin(ang)]) / np.sqrt(SEQ)
    tok = tok.reshape(2, TT, P, SEQ).transpose(2, 0, 1, 3)
    pool = np.zeros((HEADS, SEQ, SEQ))
    for g, w in enumerate(WINDOWS):
        for t in range(SEQ):
            lo, hi = max(t - w // 2, 0), min(t + w - w // 2, SEQ)
            pool[g, lo:hi, t] = 1.0 / (hi - lo)
            pool[g, t, t] -= 1.0
    pool = pool.reshape(HEADS, TT, P, SEQ).transpose(2, 0, 1, 3)
    return {"ident": np.eye(P), "dft_channels": ch, "dft_tokens": tok, "pool_matrix": pool}


def kernel(**inputs):
    import concourse.bacc as bacc
    from concourse.bass_utils import run_bass_kernel_spmd as run

    a = {k: np.asarray(v) for k, v in inputs.items()}
    L, C = LAYERS, CHUNKS

    def columns(w, tile):
        n = w.shape[2] // tile
        return w.reshape(L, KT, P, n, tile).transpose(0, 3, 2, 1, 4)

    def ffn_pairs(n):
        gate = columns(a[f"ffn{n}_w_gate"], P).reshape(L * C, P, W)
        up = columns(a[f"ffn{n}_w_up"], P).reshape(L * C, P, W)
        return np.concatenate([gate, up], axis=2)

    w_in, w_out = a["mix_w_in"], a["mix_w_out"].reshape(L, KT, P, D)
    part = [w_in[:, :, i * GROUP:(i + 1) * GROUP] for i in range(7)]
    wa, wp, wb, wc, wh, wu, wv = part
    pv = np.concatenate([wp, wv], axis=2).reshape(L, 2, 4, P, 2 * GROUP).transpose(0, 1, 3, 2, 4)
    pv = pv.reshape(L, 2, P, 2 * W)
    ta, tb, tc, th, tu = [columns(w, P).reshape(L, CT, P, W) for w in (wa, wb, wc, wh, wu)]

    def pair(m, n):
        return np.concatenate([m, n], axis=2)

    mix_pairs = np.stack([
        pv[:, 0], pv[:, 1], pair(ta[:, 0], ta[:, 1]), pair(tc[:, 0], th[:, 0]), pair(tc[:, 1], th[:, 1]),
        pair(tu[:, 0], tu[:, 1]), pair(w_out[:, 0], w_out[:, 1]), pair(w_out[:, 2], w_out[:, 3])], axis=1)
    mix_singles = np.stack([tb[:, 0], tb[:, 1], w_out[:, 4], w_out[:, 5], w_out[:, 6], w_out[:, 7]], axis=1)
    conv = a["conv_w"].reshape(L, 3, CT, P).transpose(0, 3, 1, 2)
    small = np.concatenate([a["pool_scale"].reshape(L, 1, CT, P).transpose(0, 3, 1, 2), conv], axis=2)

    def by_parity(w):
        return w.reshape(L, CT, 2, *w.shape[2:])

    arrays = {
        "x": a["x"].reshape(SEQ, D),
        "ffn_pairs": np.stack([ffn_pairs(1), ffn_pairs(2)]),
        "ffn_singles": np.stack([a["ffn1_w_down"].reshape(L * C, P, D), a["ffn2_w_down"].reshape(L * C, P, D)]),
        "mix_pairs": mix_pairs.reshape(L * MIX_PAIRS, P, 2 * W),
        "mix_singles": mix_singles.reshape(L * MIX_SINGLES, P, W),
        "ln_params": np.stack([a[f"ln{s}_{w}"] for s in (1, 2, 3) for w in "gb"], axis=1),
        "v_params": np.stack([a["gmlp_ln_g"], a["gmlp_ln_b"]], axis=1),
        "gate_bias": by_parity(a["gmlp_b_s"]).transpose(0, 2, 1, 3),
        "pool_w": by_parity(a["pool_w"]).transpose(0, 2, 3, 1, 4),
        "small": small.reshape(L, P, 4 * CT),
        "spatial_w": a["gmlp_w_s"].transpose(0, 3, 1, 2),
        **constants(),
    }
    nc = bacc.Bacc("TRN2", target_bir_lowering=False, num_devices=1)
    sent, args = {}, []
    for name, v in arrays.items():
        v = np.ascontiguousarray(v, dtype=np.float32)
        sent[name + "_dram"] = v
        args.append(nc.dram_tensor(name + "_dram", v.shape, F32, kind="ExternalInput").ap())
    args.append(nc.dram_tensor("out_dram", (SEQ, D), F32, kind="ExternalOutput").ap())
    build(nc, *args)
    r = run(nc, [sent], core_ids=[0])
    return r.results[0]["out_dram"].reshape(1, SEQ, D)
```

```python
from contextlib import ExitStack

import numpy as np

import concourse.bass as bass
from concourse import mybir

ALU = mybir.AluOpType
ACT = mybir.ActivationFunctionType
F32 = mybir.dt.float32
F32R = mybir.dt.float32r

P = 128
LAYERS = 2
SEQ = 256
D = 1024
DFF = 2816
GROUP = 256
HEADS = 4
HEAD = GROUP // HEADS
CHUNK = 128
WINDOWS = (2, 4, 8, 16)
POOL_REACH = max(WINDOWS) // 2
ALPHA = (2 * LAYERS) ** 0.25
LN_EPS = 1e-5

TT = SEQ // P
KT = D // P
HALF = D // 2
CT = GROUP // P
CHUNKS = DFF // P
W = 1024

MIX_PAIRS = 8
MIX_SINGLES = 6
PAIRS = 2 * CHUNKS + MIX_PAIRS
SINGLES = 2 * CHUNKS + MIX_SINGLES
FFN_PAIR0 = (0, CHUNKS + MIX_PAIRS)
FFN_SINGLE0 = (0, CHUNKS + MIX_SINGLES)
MIX_PAIR0 = CHUNKS
MIX_SINGLE0 = CHUNKS
LAST_SINGLE = (CHUNKS - 1, CHUNKS + MIX_SINGLES - 1, SINGLES - 1)
STAGES = 3
LN_COUNTS = 6
MIX_COUNTS = 19


def build(nc, x, ffn_pairs, ffn_singles, mix_pairs, mix_singles, ln_params, v_params, gate_bias,
          pool_w, small, spatial_w, ident_c, dft_channels, dft_tokens, pool_matrix, out):
    with ExitStack() as ctx:
        def sb(name, shape, dt=F32):
            return ctx.enter_context(nc.sbuf_tensor(name, shape, dt))

        def sem(name):
            return ctx.enter_context(nc.semaphore(name))

        raw_pair = sb("raw_pair", [P, 2, 2, W])
        raw_single = sb("raw_single", [P, 2, W])
        hi_pair = sb("hi_pair", [P, 2, 2, W], F32R)
        lo_pair = sb("lo_pair", [P, 2, 2, W], F32R)
        hi_single = sb("hi_single", [P, 2, W], F32R)
        lo_single = sb("lo_single", [P, 2, W], F32R)
        x_tok = sb("x_tok", [P, TT, D])
        xT_hi = sb("xT_hi", [P, KT, SEQ], F32R)
        xT_lo = sb("xT_lo", [P, KT, SEQ], F32R)
        res = sb("res", [P, D])
        res_hi = sb("res_hi", [P, TT, D], F32R)
        res_lo = sb("res_lo", [P, TT, D], F32R)
        silu_g = sb("silu_g", [P, 2, SEQ])
        hid = sb("hid", [P, 2, SEQ])
        hid_hi = sb("hid_hi", [P, 2, SEQ], F32R)
        hid_lo = sb("hid_lo", [P, 2, SEQ], F32R)
        centred = sb("centred", [P, 2, HALF])
        stats = sb("stats", [P, 2, 6])
        mean_var = sb("mean_var", [P, TT, 2])
        eps = sb("eps", [P, 2])
        std = sb("std", [P, TT])
        rstd = sb("rstd", [P, 1])
        ln = sb("ln", [P, 2 * STAGES, D])
        vln = sb("vln", [P, 2, GROUP])
        bias_s = sb("bias_s", [P, CT, CHUNK])
        pool_bd = sb("pool_bd", [P, CT, P])
        chan = sb("chan", [P, 4 * CT])
        ws = sb("ws", [P, HEADS, CHUNK])
        ident = sb("ident", [P, P])
        ident_r = sb("ident_r", [P, P], F32R)
        dft_ch = sb("dft_ch", [P, 2 * P])
        dft_tok = sb("dft_tok", [P, 2, 2, P])
        pool_m = sb("pool_m", [P, HEADS, TT, P + POOL_REACH])
        aT = sb("aT", [P, CT, SEQ])
        a_fold = sb("a_fold", [P, 2, CT, P])
        y1 = sb("y1", [P, TT, 2 * GROUP])
        p_tok = sb("p_tok", [P, TT, GROUP])
        pooled = aT
        v_mid = sb("v_mid", [P, GROUP])
        v_tok = sb("v_tok", [P, TT, GROUP])
        c_gate = sb("c_gate", [P, SEQ])
        z_pad = sb("z_pad", [P, SEQ + 2])
        conv = sb("conv", [P, SEQ])
        mixed = sb("mixed", [P, CT, SEQ])
        y_full = sb("y_full", [P, CT, SEQ])
        yT_hi = sb("yT_hi", [P, KT, SEQ], F32R)
        yT_lo = sb("yT_lo", [P, KT, SEQ], F32R)

        def flat(y):
            return y[:, 0:KT // 2, :].rearrange("p k n -> p (k n)")

        last_hi_single, last_lo_single = flat(yT_hi), flat(yT_lo)
        last_hid_hi, last_hid_lo = yT_hi[:, KT // 2, :], yT_lo[:, KT // 2, :]

        def by_parity(c):
            return acc[:, 1, c * SEQ:(c + 1) * SEQ].rearrange("p (q i) -> p i q", q=2)

        def in_order(y):
            return y.rearrange("p (i q) -> p i q", q=2)

        acc = ctx.enter_context(nc.psum_tensor("acc", [P, 2 * TT, HALF], F32))
        work = ctx.enter_context(nc.psum_tensor("work", [P, 4, HALF], F32))

        pair_landed = [[sem(f"pair_landed{i}{a}") for a in range(2)] for i in range(2)]
        single_landed = [sem(f"single_landed{i}") for i in range(2)]
        hi_pair_ready, hi_single_ready = sem("hi_pair_ready"), sem("hi_single_ready")
        lo_pair_ready, lo_single_ready = sem("lo_pair_ready"), sem("lo_single_ready")
        pair_used, single_used = sem("pair_used"), sem("single_used")
        x_landed = [sem(f"x_landed_{part}") for part in ("tile0_half0", "tile0_half1", "tile1")]
        x_ready = sem("x_ready")
        transposed = sem("transposed")
        xT_hi_ready, xT_lo_ready = sem("xT_hi_ready"), sem("xT_lo_ready")
        res_step, res_ready = sem("res_step"), sem("res_ready")
        silu_ready, hid_step, hid_ready = sem("silu_ready"), sem("hid_step"), sem("hid_ready")
        last_hid_step, last_hid_ready = sem("last_hid_step"), sem("last_hid_ready")
        tok_done, tok_hid_ready = sem("tok_done"), sem("tok_hid_ready")
        hid_transposed, hidT_hi_ready = sem("hid_transposed"), sem("hidT_hi_ready")
        acc_done = sem("acc_done")
        ln_step, std_ready = sem("ln_step"), sem("std_ready")
        const_landed, ident_landed = sem("const_landed"), sem("ident_landed")
        ident_ready, bd_zeroed, pad_zeroed = sem("ident_ready"), sem("bd_zeroed"), sem("pad_zeroed")
        eps_written = sem("eps_written")
        params_landed = sem("params_landed")
        mix_step = sem("mix_step")
        p_ready, aT_ready, y1_ready = sem("p_ready"), sem("aT_ready"), sem("y1_ready")
        a_folded = sem("a_folded")
        v_var_ready, v_std_ready, v_ready = sem("v_var_ready"), sem("v_std_ready"), sem("v_ready")
        c_ready, z_ready = sem("c_ready"), sem("z_ready")
        dft1_done, pool_done, dft2_done = sem("dft1_done"), sem("pool_done"), sem("dft2_done")
        pooled_ready, pool_w_done, scaled_ready = sem("pooled_ready"), sem("pool_w_done"), sem("scaled_ready")
        spatial_done, mixed_ready = sem("spatial_done"), sem("mixed_ready")
        ya_hi_ready, ya_ready, yb_ready = sem("ya_hi_ready"), sem("ya_ready"), sem("yb_ready")
        yc_ready, yd_ready = sem("yc_ready"), sem("yd_ready")
        stored = sem("stored")
        dve_passed, pool_passed = sem("dve_passed"), sem("pool_passed")

        FREE_PAIR_TILES = 4
        FREE_SINGLES = 2
        PARAM_LOADS = 9
        CONST_LOADS = 3

        def pair_tiles(l, n, i=0):
            return (2 * PAIRS) * l + 2 * n + 4 * i

        def singles(l, n, i=0):
            return SINGLES * l + n + 2 * i

        def pair_loads(l, n, i=0):
            return (PAIRS // 2) * l + n // 2 + i

        def single_loads(l, n, i=0):
            return (SINGLES // 2) * l + n // 2 + i

        def part(a, halved):
            if halved:
                return slice(None), slice(None), slice(a * HALF, (a + 1) * HALF)
            return slice(None), a, slice(None)

        block = ctx.enter_context(nc.Block())

        @block.sync
        def _(sp):
            def load_pair(l, n, src, i=0, halved=False):
                sp.wait_ge(lo_pair_ready, pair_tiles(l, n, i) - 2 + FREE_PAIR_TILES)
                src = src.rearrange("p (b w) -> p b w", b=2)
                for a in range(2):
                    at = part(a, halved)
                    sp.dma_start(raw_pair[:, n % 2, :, :][at], src[at]).then_inc(pair_landed[n % 2][a], 16)

            def load_single(l, n, src, i=0):
                sp.wait_ge(lo_single_ready, singles(l, n, i) - 1 + FREE_SINGLES)
                sp.dma_start(raw_single[:, n % 2, :], src).then_inc(single_landed[n % 2], 16)

            def ffn_pair(l, f, j, i=0):
                load_pair(l, FFN_PAIR0[f] + j, ffn_pairs[(l * CHUNKS + f * LAYERS * CHUNKS + j) + 2 * i], i,
                          halved=j == 0)

            def next_layer_pair(l, j):
                load_pair(l, PAIRS + j, ffn_pairs[(l + 1) * CHUNKS + j], halved=j == 0)

            def ffn_single(l, f, j, i=0):
                load_single(l, FFN_SINGLE0[f] + j, ffn_singles[f, (l * CHUNKS + j) + 2 * i], i)

            def mix_pair(l, g):
                load_pair(l, MIX_PAIR0 + g, mix_pairs[l * MIX_PAIRS + g])

            def mix_single(l, g):
                load_single(l, MIX_SINGLE0 + g, mix_singles[l * MIX_SINGLES + g])

            for h in range(2):
                cols = slice(h * HALF, (h + 1) * HALF)
                sp.dma_start(x_tok[:, 0, cols], x[0:P, cols]).then_inc(x_landed[h], 16)
            ffn_pair(0, 0, 0)
            ffn_pair(0, 0, 1)
            with sp.Fori(0, LAYERS) as l:
                ffn_single(l, 0, 0)
                with sp.Fori(0, (CHUNKS - 2) // 2) as i:
                    for j in (2, 3):
                        ffn_pair(l, 0, j, i)
                        ffn_single(l, 0, j - 1, i)
                mix_pair(l, 0)
                ffn_single(l, 0, CHUNKS - 1)
                mix_pair(l, 1)
                mix_single(l, 0)
                mix_single(l, 1)
                for g in (2, 3, 4, 5):
                    mix_pair(l, g)
                mix_single(l, 2)
                mix_pair(l, 6)
                mix_single(l, 3)
                mix_pair(l, 7)
                mix_single(l, 4)
                mix_single(l, 5)
                ffn_pair(l, 1, 0)
                ffn_pair(l, 1, 1)
                ffn_single(l, 1, 0)
                with sp.Fori(0, (CHUNKS - 2) // 2) as i:
                    for j in (2, 3):
                        ffn_pair(l, 1, j, i)
                        ffn_single(l, 1, j - 1, i)
                next_layer_pair(l, 0)
                ffn_single(l, 1, CHUNKS - 1)
                next_layer_pair(l, 1)
            for t in range(TT):
                for h in range(2):
                    cols = slice(h * HALF, (h + 1) * HALF)
                    sp.wait_ge(x_ready, 2 * TT * (STAGES * LAYERS) + 2 * t + h + 1)
                    sp.dma_start(out[t * P:(t + 1) * P, cols], x_tok[:, t, cols]).then_inc(stored, 16)
            sp.wait_ge(stored, 16 * 2 * TT)

        @block.gpsimd
        def _(pool):
            nc.gpsimd.memset(pool_bd[:, :, :], 0.0).then_inc(bd_zeroed, 1)
            nc.gpsimd.memset(z_pad[:, :], 0.0).then_inc(pad_zeroed, 1)
            nc.gpsimd.memset(eps[:, 0:1], LN_EPS).then_inc(eps_written, 1)
            nc.gpsimd.memset(eps[:, 1:2], 4 * LN_EPS).then_inc(eps_written, 1)
            for h in range(2):
                pool.wait_ge(x_landed[h], 16)
                nc.gpsimd.sem_inc(x_ready, 1)
            pool.wait_ge(pair_landed[0][0], 16)
            pool.dma_start(x_tok[:, 1, :], x[P:2 * P, :]).then_inc(x_landed[2], 16)
            pool.wait_ge(x_landed[2], 16)
            nc.gpsimd.sem_inc(x_ready, 2)

            def residual(l, s):
                scale = ALPHA if s == 1 else 2 * ALPHA
                for t in range(TT):
                    n = TT * STAGES * l + TT * s + t
                    pool.wait_ge(x_ready, 2 * n + 2)
                    nc.gpsimd.sem_inc(pool_passed, 1)
                    nc.gpsimd.tensor_scalar(res_hi[:, t, :], x_tok[:, t, :], scale, 0.0, ALU.mult, ALU.add)\
                        .then_inc(res_step, 1)
                    if t > 0:
                        pool.wait_ge(res_ready, n)
                        nc.gpsimd.sem_inc(pool_passed, 1)
                    nc.gpsimd.tensor_scalar(res[:, :], x_tok[:, t, :], scale, 0.0, ALU.mult, ALU.add)\
                        .then_inc(res_step, 1)
                    pool.wait_ge(res_step, 2 * n + 2)
                    nc.gpsimd.tensor_tensor(res_lo[:, t, :], res[:, :], res_hi[:, t, :].bitcast(F32),
                                            ALU.subtract).then_inc(res_ready, 1)

            def lo_of_late_tile(l, n):
                pool.wait_ge(hi_pair_ready, pair_tiles(l, n) + 2)
                pool.wait_ge(lo_pair_ready, pair_tiles(l, n) + 1 + FREE_PAIR_TILES)
                nc.gpsimd.tensor_tensor(lo_pair[:, n % 2, 1, :], raw_pair[:, n % 2, 1, :],
                                        hi_pair[:, n % 2, 1, :].bitcast(F32), ALU.subtract)\
                    .then_inc(lo_pair_ready, 1)

            pool.wait_ge(bd_zeroed, 1)
            with pool.Fori(0, LAYERS) as l:
                residual(l, 0)
                pool.dma_start(ln[:, :, :], ln_params[l].partition_broadcast(P)).then_inc(params_landed, 16)
                pool.dma_start(vln[:, :, :], v_params[l].partition_broadcast(P)).then_inc(params_landed, 16)
                for hh in range(2):
                    at = slice(hh * HEAD, (hh + 1) * HEAD)
                    pool.dma_start(bias_s[at, :, :], gate_bias[l, hh].partition_broadcast(HEAD))\
                        .then_inc(params_landed, 16)
                    pool.dma_start(pool_bd[at, :, at], pool_w[l, hh]).then_inc(params_landed, 16)
                pool.dma_start(chan[:, :], small[l]).then_inc(params_landed, 16)
                pool.dma_start(ws[:, 0:2, :], spatial_w[l, :, 0:2, :]).then_inc(params_landed, 16)
                pool.dma_start(ws[:, 2:4, :], spatial_w[l, :, 2:4, :]).then_inc(params_landed, 16)
                lo_of_late_tile(l, MIX_PAIR0 + 1)
                residual(l, 1)
                lo_of_late_tile(l, FFN_PAIR0[1] + 1)
                residual(l, 2)
                lo_of_late_tile(l, PAIRS + 1)

        @block.scalar
        def _(act):
            def copy(dst, src):
                return nc.scalar.activation(dst, src, ACT.Copy)

            def hi_of_pair(l, n, i=0, halved=False, parts=(0, 1)):
                for a in parts:
                    act.wait_ge(pair_landed[n % 2][a], 16 * pair_loads(l, n, i) + 16)
                    act.wait_ge(pair_used, pair_tiles(l, n, i) - (2 if halved else 3 - a) + FREE_PAIR_TILES)
                    at = part(a, halved)
                    copy(hi_pair[:, n % 2, :, :][at], raw_pair[:, n % 2, :, :][at]).then_inc(hi_pair_ready, 1)

            def hi_of_single(l, n, i=0):
                act.wait_ge(single_landed[n % 2], 16 * single_loads(l, n, i) + 16)
                act.wait_ge(single_used, singles(l, n, i) - 1 + FREE_SINGLES)
                copy(hi_single[:, n % 2, :], raw_single[:, n % 2, :]).then_inc(hi_single_ready, 1)

            def hi_of_last_single(l, f):
                n = FFN_SINGLE0[f] + CHUNKS - 1
                act.wait_ge(single_landed[n % 2], 16 * single_loads(l, n) + 16)
                copy(last_hi_single, raw_single[:, n % 2, :]).then_inc(hi_single_ready, 1)

            def spread(l, s, t):
                for h in range(2):
                    n = 2 * TT * STAGES * l + 2 * TT * s + 2 * t + h
                    act.wait_ge(transposed, n + 1)
                    copy(xT_hi[:, 4 * h:4 * h + 4, t * P:(t + 1) * P],
                         acc[:, 2 * t + h, :].rearrange("p (k n) -> p k n", k=4)).then_inc(xT_hi_ready, 1)

            def deviation(l, s, t):
                act.wait_ge(ln_step, LN_COUNTS * (TT * STAGES * l + TT * s + t) + 3)
                which = 0 if s == 1 else 1
                nc.scalar.activation(std[:, t:t + 1], mean_var[:, t, 1:2], ACT.Sqrt,
                                     bias=eps[:, which:which + 1]).then_inc(std_ready, 1)

            def between_stages(l, s, after_deviation=lambda: None):
                deviation(l, s, 0)
                after_deviation()
                spread(l, s + 1, 0)
                deviation(l, s, 1)
                if s < STAGES - 1:
                    spread(l, s + 1, 1)

            def silu(l, f, j, i=0):
                act.wait_ge(pair_used, pair_tiles(l, FFN_PAIR0[f] + j, i) + 1 + FREE_PAIR_TILES)
                nc.scalar.activation(silu_g[:, j % 2, :], work[:, 2 * (j % 2), 0:SEQ], ACT.Silu)\
                    .then_inc(silu_ready, 1)

            def silu_tok(l, f, j, t):
                if t == 0:
                    act.wait_ge(tok_done, 4 * l + 2 * f + j + 1)
                else:
                    act.wait_ge(pair_used, pair_tiles(l, FFN_PAIR0[f] + j) + 2 + FREE_PAIR_TILES)
                nc.scalar.activation(silu_g[:, j, t * P:(t + 1) * P], work[:, 2 * j + t, 0:P], ACT.Silu)\
                    .then_inc(silu_ready, 1)

            def hidT_hi(l, f, j):
                act.wait_ge(hid_transposed, 4 * l + 2 * f + j + 1)
                copy(hid_hi[:, j, :], work[:, 2 * j, 0:SEQ]).then_inc(hidT_hi_ready, 1)

            def ffn(l, f, after_silu_before_last, after_last_silu):
                def step(j, i=0):
                    silu(l, f, j, i)
                    hi_of_pair(l, FFN_PAIR0[f] + j + 2, i)
                    hi_of_single(l, FFN_SINGLE0[f] + j + 1, i)

                silu_tok(l, f, 0, 0)
                silu_tok(l, f, 1, 0)
                hi_of_single(l, FFN_SINGLE0[f] + 1)
                silu_tok(l, f, 0, 1)
                hi_of_pair(l, FFN_PAIR0[f] + 2)
                silu_tok(l, f, 1, 1)
                hidT_hi(l, f, 0)
                hi_of_pair(l, FFN_PAIR0[f] + 3)
                hidT_hi(l, f, 1)
                hi_of_single(l, FFN_SINGLE0[f] + 2)
                with act.Fori(0, (CHUNKS - 4) // 2) as i:
                    step(2, i)
                    step(3, i)
                silu(l, f, CHUNKS - 2)
                after_silu_before_last()
                silu(l, f, CHUNKS - 1)
                after_last_silu()

            act.dma_start(ident[:, :], ident_c).then_inc(ident_landed, 16)
            act.wait_ge(ident_landed, 16)
            copy(ident_r[:, :], ident[:, :]).then_inc(ident_ready, 1)
            act.wait_ge(eps_written, 2)
            spread(0, 0, 0)
            hi_of_pair(0, 0, halved=True)
            hi_of_pair(0, 1)
            act.dma_start(dft_ch[:, :], dft_channels).then_inc(const_landed, 16)
            act.dma_start(dft_tok[:, :, :, :], dft_tokens).then_inc(const_landed, 16)
            act.dma_start(pool_m[:, :, :, :], pool_matrix).then_inc(const_landed, 16)
            with act.Fori(0, LAYERS) as l:
                spread(l, 0, 1)
                hi_of_single(l, 0)

                def mix_pair(g):
                    hi_of_pair(l, MIX_PAIR0 + g)

                def mix_single(g):
                    hi_of_single(l, MIX_SINGLE0 + g)

                def into_mixer_0():
                    mix_pair(0)
                    hi_of_last_single(l, 0)

                def into_mixer_1():
                    mix_pair(1)

                def into_next_layer_0():
                    hi_of_pair(l, PAIRS, halved=True)
                    hi_of_last_single(l, 1)

                def into_next_layer_1():
                    hi_of_pair(l, PAIRS + 1)

                ffn(l, 0, into_mixer_0, into_mixer_1)
                between_stages(l, 0)

                mix_single(0)
                mix_single(1)
                mix_pair(2)
                mix_pair(3)
                for t in range(TT):
                    act.wait_ge(pair_used, pair_tiles(l, MIX_PAIR0 + 2) + FREE_PAIR_TILES)
                    copy(p_tok[:, t, :], acc[:, t, 0:GROUP]).then_inc(p_ready, 1)
                for t in range(TT):
                    act.wait_ge(v_var_ready, TT * l + t + 1)
                    nc.scalar.activation(std[:, t:t + 1], mean_var[:, t, 1:2], ACT.Sqrt, bias=eps[:, 0:1])\
                        .then_inc(v_std_ready, 1)
                act.wait_ge(pair_used, pair_tiles(l, MIX_PAIR0 + 3) + FREE_PAIR_TILES)
                copy(aT[:, :, :], work[:, 0, :].rearrange("p (c n) -> p c n", c=CT)).then_inc(aT_ready, 1)
                mix_pair(4)
                act.wait_ge(pair_used, pair_tiles(l, MIX_PAIR0 + 4) + FREE_PAIR_TILES)
                copy(c_gate[:, :], work[:, 1, 0:SEQ]).then_inc(c_ready, 1)
                mix_pair(5)
                for q in range(2):
                    act.wait_ge(dft1_done, 2 * l + q + 1)
                    copy(y1[:, q, :], acc[:, TT + q, :]).then_inc(y1_ready, 1)
                mix_single(2)
                act.wait_ge(pair_used, pair_tiles(l, MIX_PAIR0 + 5) + FREE_PAIR_TILES)
                act.wait_ge(z_ready, CT * l + 1)
                copy(c_gate[:, :], work[:, 3, 0:SEQ]).then_inc(c_ready, 1)
                mix_pair(6)
                act.wait_ge(pool_done, l + 1)
                copy(pooled[:, :, :], work[:, 0, :].rearrange("p (c n) -> p c n", c=CT))\
                    .then_inc(pooled_ready, 1)
                mix_single(3)
                act.wait_ge(dft2_done, l + 1)
                for c in range(CT):
                    copy(in_order(yT_hi[:, c, :]), by_parity(c)).then_inc(ya_hi_ready, 1)
                mix_pair(7)
                act.wait_ge(pool_w_done, l + 1)
                act.wait_ge(yc_ready, CT * l + CT)
                for c in range(CT):
                    nc.scalar.activation(y_full[:, c, :], work[:, 3, c * SEQ:(c + 1) * SEQ], ACT.Copy,
                                         scale=chan[:, c:c + 1]).then_inc(scaled_ready, 1)
                mix_single(4)
                mix_single(5)
                hi_of_pair(l, FFN_PAIR0[1], halved=True)
                hi_of_pair(l, FFN_PAIR0[1] + 1, parts=(0,))
                between_stages(l, 1, after_deviation=lambda: hi_of_pair(l, FFN_PAIR0[1] + 1, parts=(1,)))
                hi_of_single(l, FFN_SINGLE0[1])

                ffn(l, 1, into_next_layer_0, into_next_layer_1)
                between_stages(l, 2)

        @block.vector
        def _(dve):
            def lo_of_pair(l, n, i=0, parts=(0, 1), halved=False):
                for a in parts:
                    dve.wait_ge(hi_pair_ready, pair_tiles(l, n, i) + a + 1)
                    at = part(a, halved)
                    nc.vector.tensor_tensor(lo_pair[:, n % 2, :, :][at], raw_pair[:, n % 2, :, :][at],
                                            hi_pair[:, n % 2, :, :][at].bitcast(F32), ALU.subtract)\
                        .then_inc(lo_pair_ready, 1)

            def late_tile_done(l, n):
                dve.wait_ge(lo_pair_ready, pair_tiles(l, n) + 2 + FREE_PAIR_TILES)

            def lo_of_single(l, n, i=0):
                dve.wait_ge(hi_single_ready, singles(l, n, i) + 1)
                nc.vector.tensor_tensor(lo_single[:, n % 2, :], raw_single[:, n % 2, :],
                                        hi_single[:, n % 2, :].bitcast(F32), ALU.subtract)\
                    .then_inc(lo_single_ready, 1)

            def lo_of_last_single(l, f):
                n = FFN_SINGLE0[f] + CHUNKS - 1
                dve.wait_ge(hi_single_ready, singles(l, n) + 1)
                nc.vector.tensor_tensor(last_lo_single, raw_single[:, n % 2, :], last_hi_single.bitcast(F32),
                                        ALU.subtract).then_inc(lo_single_ready, 1)

            def spread(l, s, t, halves=(0, 1)):
                for h in halves:
                    dve.wait_ge(xT_hi_ready, 2 * TT * STAGES * l + 2 * TT * s + 2 * t + h + 1)
                    at = (slice(None), slice(4 * h, 4 * h + 4), slice(t * P, (t + 1) * P))
                    nc.vector.tensor_tensor(xT_lo[at],
                                            acc[:, 2 * t + h, :].rearrange("p (k n) -> p k n", k=4),
                                            xT_hi[at].bitcast(F32), ALU.subtract).then_inc(xT_lo_ready, 1)

            def norm_stats(l, s, t, before_half=lambda h: None):
                step = LN_COUNTS * (TT * STAGES * l + TT * s + t)
                for h in range(2):
                    before_half(h)
                    if 2 * t + h < 2 * TT - 1:
                        dve.wait_ge(acc_done, (2 * TT - 1) * (STAGES * l + s) + 2 * t + h + 1)
                    else:
                        dve.wait_ge(single_used, singles(l, LAST_SINGLE[s]) + 1 + FREE_SINGLES)
                    nc.vector.bn_stats(stats[:, h, :], acc[:, 2 * t + h, :]).then_inc(ln_step, 1)
                dve.wait_ge(ln_step, step + 2)
                nc.vector.sem_inc(dve_passed, 1)
                nc.vector.bn_aggr(mean_var[:, t, :], stats[:, :, :].rearrange("p a b -> p (a b)"))\
                    .then_inc(ln_step, 1)

            def norm_apply(l, s, t):
                n = TT * STAGES * l + TT * s + t
                step = LN_COUNTS * n
                if s == 0 and t == 0:
                    dve.wait_ge(params_landed, 16 * PARAM_LOADS * (l + 1))
                dve.wait_ge(ln_step, step + 3)
                for h in range(2):
                    cols = slice(h * HALF, (h + 1) * HALF)
                    nc.vector.scalar_tensor_tensor(centred[:, h, :], acc[:, 2 * t + h, :], mean_var[:, t, 0:1],
                                                   ln[:, 2 * s, cols], ALU.subtract, ALU.mult)\
                        .then_inc(ln_step, 1)
                    if h == 0:
                        dve.wait_ge(std_ready, n + 1)
                        nc.vector.reciprocal(rstd[:, :], std[:, t:t + 1]).then_inc(ln_step, 1)
                    dve.wait_ge(ln_step, step + 5 + h)
                    nc.vector.scalar_tensor_tensor(x_tok[:, t, cols], centred[:, h, :], rstd[:, :],
                                                   ln[:, 2 * s + 1, cols], ALU.mult, ALU.add)\
                        .then_inc(x_ready, 1)

            def between_stages(l, s):
                norm_stats(l, s, 0)
                norm_apply(l, s, 0)
                norm_stats(l, s, 1, before_half=lambda h: spread(l, s + 1, 0, halves=(h,)))
                norm_apply(l, s, 1)
                if s < STAGES - 1:
                    spread(l, s + 1, 1)

            def hidden_tok(l, f, j, t):
                dve.wait_ge(silu_ready, (CHUNKS + 2) * (2 * l + f) + 2 * t + j + 1)
                toks = slice(t * P, (t + 1) * P)
                nc.vector.tensor_tensor(hid[:, j, toks], silu_g[:, j, toks], work[:, 2 * j + t, P:2 * P],
                                        ALU.mult).then_inc(tok_hid_ready, 1)

            def hidT_lo(l, f, j):
                dve.wait_ge(hidT_hi_ready, 4 * l + 2 * f + j + 1)
                nc.vector.tensor_tensor(hid_lo[:, j, :], work[:, 2 * j, 0:SEQ], hid_hi[:, j, :].bitcast(F32),
                                        ALU.subtract).then_inc(hid_ready, 1)

            def hidden(l, f, j, i=0):
                n = (CHUNKS - 3) * (2 * l + f) + j - 2 + 2 * i
                dve.wait_ge(pair_used, pair_tiles(l, FFN_PAIR0[f] + j, i) + 2 + FREE_PAIR_TILES)
                dve.wait_ge(silu_ready, (CHUNKS + 2) * (2 * l + f) + j + 2 * i + 3)
                b = j % 2
                up = work[:, 2 * b + 1, 0:SEQ]
                nc.vector.tensor_tensor(hid[:, b, :], silu_g[:, b, :], up, ALU.mult).then_inc(hid_step, 1)
                dve.wait_ge(hid_step, 2 * n + 1)
                nc.vector.tensor_copy(hid_hi[:, b, :], hid[:, b, :]).then_inc(hid_step, 1)
                dve.wait_ge(hid_step, 2 * n + 2)
                nc.vector.tensor_tensor(hid_lo[:, b, :], hid[:, b, :], hid_hi[:, b, :].bitcast(F32),
                                        ALU.subtract).then_inc(hid_ready, 1)

            def last_hidden(l, f):
                j, n = CHUNKS - 1, 2 * l + f
                b = j % 2
                dve.wait_ge(pair_used, pair_tiles(l, FFN_PAIR0[f] + j) + 2 + FREE_PAIR_TILES)
                dve.wait_ge(silu_ready, (CHUNKS + 2) * n + j + 3)
                for t in range(TT):
                    toks = slice(t * P, (t + 1) * P)
                    nc.vector.tensor_tensor(hid[:, b, toks], silu_g[:, b, toks],
                                            work[:, 2 * b + 1, toks], ALU.mult).then_inc(last_hid_step, 1)
                    dve.wait_ge(last_hid_step, 2 * TT * n + 2 * t + 1)
                    nc.vector.tensor_copy(last_hid_hi[:, toks], hid[:, b, toks]).then_inc(last_hid_step, 1)
                    dve.wait_ge(last_hid_step, 2 * TT * n + 2 * t + 2)
                    nc.vector.tensor_tensor(last_hid_lo[:, toks], hid[:, b, toks],
                                            last_hid_hi[:, toks].bitcast(F32), ALU.subtract)\
                        .then_inc(last_hid_ready if t == 0 else hid_ready, 1)

            def ffn(l, f, after_hidden_before_last, before_last_hidden):
                def step(j, i=0):
                    hidden(l, f, j, i)
                    lo_of_pair(l, FFN_PAIR0[f] + j + 2, i)
                    lo_of_single(l, FFN_SINGLE0[f] + j + 1, i)

                hidden_tok(l, f, 0, 0)
                hidden_tok(l, f, 1, 0)
                hidden_tok(l, f, 0, 1)
                lo_of_single(l, FFN_SINGLE0[f] + 1)
                late_tile_done(l, FFN_PAIR0[f] + 1)
                lo_of_pair(l, FFN_PAIR0[f] + 2, parts=(0,))
                hidden_tok(l, f, 1, 1)
                hidT_lo(l, f, 0)
                lo_of_pair(l, FFN_PAIR0[f] + 2, parts=(1,))
                lo_of_pair(l, FFN_PAIR0[f] + 3)
                hidT_lo(l, f, 1)
                lo_of_single(l, FFN_SINGLE0[f] + 2)
                with dve.Fori(0, (CHUNKS - 4) // 2) as i:
                    step(2, i)
                    step(3, i)
                hidden(l, f, CHUNKS - 2)
                after_hidden_before_last()
                before_last_hidden()
                last_hidden(l, f)

            nc.vector.sem_inc(lo_pair_ready, FREE_PAIR_TILES)
            nc.vector.sem_inc(lo_single_ready, FREE_SINGLES)
            dve.wait_ge(pad_zeroed, 1)

            spread(0, 0, 0)
            lo_of_pair(0, 0, halved=True)
            lo_of_pair(0, 1)
            with dve.Fori(0, LAYERS) as l:
                spread(l, 0, 1)
                lo_of_single(l, 0)

                def mix_pair(g):
                    lo_of_pair(l, MIX_PAIR0 + g)

                def mix_single(g):
                    lo_of_single(l, MIX_SINGLE0 + g)

                def into_mixer_0():
                    mix_pair(0)
                    lo_of_last_single(l, 0)

                def into_mixer_1():
                    lo_of_pair(l, MIX_PAIR0 + 1, parts=(0,))

                def into_next_layer_0():
                    lo_of_pair(l, PAIRS, halved=True)
                    lo_of_last_single(l, 1)

                def into_next_layer_1():
                    lo_of_pair(l, PAIRS + 1, parts=(0,))

                ffn(l, 0, into_mixer_0, into_mixer_1)
                between_stages(l, 0)

                count = [0]

                def chain(ins):
                    count[0] += 1
                    ins.then_inc(mix_step, 1)
                    dve.wait_ge(mix_step, MIX_COUNTS * l + count[0])

                mix_single(0)
                mix_single(1)
                late_tile_done(l, MIX_PAIR0 + 1)
                mix_pair(2)
                mix_pair(3)
                dve.wait_ge(pair_used, pair_tiles(l, MIX_PAIR0 + 2) + FREE_PAIR_TILES)
                for t in range(TT):
                    dve.wait_ge(p_ready, TT * l + t + 1)
                    v = acc[:, t, GROUP:2 * GROUP]
                    chain(nc.vector.bn_stats(stats[:, 0, :], v))
                    nc.vector.sem_inc(dve_passed, 1)
                    nc.vector.bn_aggr(mean_var[:, t, :], stats[:, 0, :]).then_inc(v_var_ready, 1)
                    dve.wait_ge(v_var_ready, TT * l + t + 1)
                    chain(nc.vector.scalar_tensor_tensor(v_mid[:, :], v, mean_var[:, t, 0:1], vln[:, 0, :],
                                                         ALU.subtract, ALU.mult))
                    dve.wait_ge(v_std_ready, TT * l + t + 1)
                    chain(nc.vector.reciprocal(rstd[:, :], std[:, t:t + 1]))
                    nc.vector.scalar_tensor_tensor(v_tok[:, t, :], v_mid[:, :], rstd[:, :], vln[:, 1, :],
                                                   ALU.mult, ALU.add).then_inc(v_ready, 1)
                dve.wait_ge(aT_ready, l + 1)
                for q, op in enumerate((ALU.add, ALU.subtract)):
                    nc.vector.tensor_tensor(a_fold[:, q, :, :], aT[:, :, 0:P], aT[:, :, P:2 * P], op)\
                        .then_inc(a_folded, 1)
                mix_pair(4)

                def conv_group(c, h_at, b_at):
                    dve.wait_ge(c_ready, CT * l + c + 1)
                    nc.vector.tensor_tensor(z_pad[:, 1:SEQ + 1], c_gate[:, :], h_at, ALU.mult).then_inc(z_ready, 1)
                    dve.wait_ge(z_ready, CT * l + c + 1)

                    def w(k):
                        return chan[:, CT * (k + 1) + c:CT * (k + 1) + c + 1]

                    chain(nc.vector.tensor_scalar(conv[:, :], z_pad[:, 0:SEQ], w(0), None, ALU.mult))
                    for k in (1, 2):
                        chain(nc.vector.scalar_tensor_tensor(conv[:, :], z_pad[:, k:k + SEQ], w(k), conv[:, :],
                                                             ALU.mult, ALU.add))
                    dve.wait_ge(single_used, singles(l, MIX_SINGLE0 + c) + 1 + FREE_SINGLES)
                    chain(nc.vector.tensor_tensor(y_full[:, c, :], conv[:, :], b_at, ALU.mult))
                    chain(nc.vector.tensor_copy(yT_hi[:, 4 + c, :], y_full[:, c, :]))
                    nc.vector.tensor_tensor(yT_lo[:, 4 + c, :], y_full[:, c, :], yT_hi[:, 4 + c, :].bitcast(F32),
                                            ALU.subtract).then_inc(yc_ready, 1)

                conv_group(0, work[:, 1, SEQ:2 * SEQ], work[:, 2, 0:SEQ])
                mix_pair(5)
                mix_single(2)
                conv_group(1, work[:, 3, SEQ:2 * SEQ], work[:, 2, SEQ:2 * SEQ])
                mix_pair(6)
                dve.wait_ge(spatial_done, l + 1)
                for c in range(CT):
                    last = nc.vector.tensor_tensor(
                        mixed[:, c, :].rearrange("p (t q) -> p t q", t=TT),
                        acc[:, 0, c * SEQ:(c + 1) * SEQ].rearrange("p (t q) -> p t q", t=TT),
                        bias_s[:, c, :].unsqueeze(1).to_broadcast([P, TT, CHUNK]), ALU.add)
                    last.then_inc(mixed_ready, 1)
                mix_single(3)
                dve.wait_ge(ya_hi_ready, CT * (l + 1))
                for c in range(CT):
                    nc.vector.tensor_tensor(in_order(yT_lo[:, c, :]), by_parity(c),
                                            in_order(yT_hi[:, c, :]).bitcast(F32), ALU.subtract)\
                        .then_inc(ya_ready, 1)
                mix_pair(7)
                dve.wait_ge(scaled_ready, CT * (l + 1))
                chain(nc.vector.tensor_copy(yT_hi[:, 2:4, :], y_full[:, :, :]))
                nc.vector.tensor_tensor(yT_lo[:, 2:4, :], y_full[:, :, :], yT_hi[:, 2:4, :].bitcast(F32),
                                        ALU.subtract).then_inc(yb_ready, 1)
                mix_single(4)
                dve.wait_ge(pair_used, pair_tiles(l, MIX_PAIR0 + 6) + FREE_PAIR_TILES)
                dve.wait_ge(mixed_ready, CT * (l + 1))
                dve.wait_ge(yb_ready, l + 1)
                chain(nc.vector.tensor_tensor(y_full[:, :, :], mixed[:, :, :],
                                              work[:, 1, :].rearrange("p (c n) -> p c n", c=CT), ALU.mult))
                chain(nc.vector.tensor_copy(yT_hi[:, 6:8, :], y_full[:, :, :]))
                nc.vector.tensor_tensor(yT_lo[:, 6:8, :], y_full[:, :, :], yT_hi[:, 6:8, :].bitcast(F32),
                                        ALU.subtract).then_inc(yd_ready, 1)
                assert count[0] == MIX_COUNTS, count
                mix_single(5)
                lo_of_pair(l, FFN_PAIR0[1], halved=True)
                lo_of_pair(l, FFN_PAIR0[1] + 1, parts=(0,))
                between_stages(l, 1)
                lo_of_single(l, FFN_SINGLE0[1])

                ffn(l, 1, into_next_layer_0, into_next_layer_1)
                between_stages(l, 2)

        @block.tensor
        def _(pe):
            def exact(dst, w_hi, w_lo, m_hi, m_lo, first, last):
                nc.tensor.matmul(dst, w_hi, m_hi, start=first, stop=False)
                nc.tensor.matmul(dst, w_hi, m_lo, start=False, stop=False)
                return nc.tensor.matmul(dst, w_lo, m_hi, start=False, stop=last)

            def transpose_x(l, s, t, halves=(0, 1)):
                for h in halves:
                    n = 2 * TT * STAGES * l + 2 * TT * s + 2 * t + h
                    pe.wait_ge(x_ready, n + 1)
                    for k in range(4):
                        col = h * HALF + k * P
                        last = nc.tensor.transpose(acc[:, 2 * t + h, k * P:(k + 1) * P],
                                                   x_tok[:, t, col:col + P], ident[:, :])
                    last.then_inc(transposed, 1)

            def spread_done(l, s, t, k):
                if k % 4 == 0:
                    pe.wait_ge(xT_lo_ready, 2 * TT * STAGES * l + 2 * TT * s + 2 * t + k // 4 + 1)

            def residual(l, s):
                for t in range(TT):
                    pe.wait_ge(res_ready, TT * STAGES * l + TT * s + t + 1)
                    for h in range(2):
                        cols = slice(h * HALF, (h + 1) * HALF)
                        nc.tensor.matmul(acc[:, 2 * t + h, :], ident_r[:, :], res_hi[:, t, cols],
                                         start=True, stop=False)
                        nc.tensor.matmul(acc[:, 2 * t + h, :], ident_r[:, :], res_lo[:, t, cols],
                                         start=False, stop=False)

            def channels_major(l, n, a, dst, i=0):
                pe.wait_ge(lo_pair_ready, pair_tiles(l, n, i) + a + 1 + FREE_PAIR_TILES)
                for k in range(KT):
                    at = slice(k * P, (k + 1) * P)
                    last = exact(dst, hi_pair[:, n % 2, a, at], lo_pair[:, n % 2, a, at],
                                 xT_hi[:, k, :], xT_lo[:, k, :], k == 0, k == KT - 1)
                last.then_inc(pair_used, 1)

            def gate_up(l, f, j, i=0):
                for a in range(2):
                    channels_major(l, FFN_PAIR0[f] + j, a, work[:, 2 * (j % 2) + a, 0:SEQ], i)

            def gate_up_tok(l, f, j, t, before=lambda k: None):
                n = FFN_PAIR0[f] + j
                toks = slice(t * P, (t + 1) * P)
                for k in range(KT):
                    before(k)
                    if t == 0 and (j, k) in ((0, 0), (0, 4), (1, 0)):
                        parts = 1 if (j, k) == (0, 0) else 2
                        pe.wait_ge(lo_pair_ready, pair_tiles(l, n) + parts + FREE_PAIR_TILES)
                    if j == 0:
                        spread_done(l, 2 * f, t, k)
                    at = slice(k * P, (k + 1) * P)
                    last = exact(work[:, 2 * j + t, 0:2 * P], xT_hi[:, k, toks], xT_lo[:, k, toks],
                                 hi_pair[:, n % 2, :, at], lo_pair[:, n % 2, :, at], k == 0, k == KT - 1)
                if t == 0:
                    last.then_inc(tok_done, 1)
                else:
                    last.then_inc(pair_used, 2)

            def transpose_hidden(l, f, j):
                for t in range(TT):
                    pe.wait_ge(tok_hid_ready, 8 * l + 4 * f + 2 * t + j + 1)
                for t in range(TT):
                    toks = slice(t * P, (t + 1) * P)
                    last = nc.tensor.transpose(work[:, 2 * j, toks], hid[:, j, toks], ident[:, :])
                last.then_inc(hid_transposed, 1)

            def first_chunks(l, f):
                s = 2 * f

                def second_x(k):
                    if k in (4, 7):
                        transpose_x(l, s, 1, halves=(0 if k == 4 else 1,))

                gate_up_tok(l, f, 0, 0)
                gate_up_tok(l, f, 1, 0, before=second_x)
                gate_up_tok(l, f, 0, 1)
                gate_up_tok(l, f, 1, 1)
                transpose_hidden(l, f, 0)
                residual(l, s)
                transpose_hidden(l, f, 1)

            def down(l, f, j, i=0, tiles=(0, 1)):
                n = FFN_SINGLE0[f] + j
                pe.wait_ge(lo_single_ready, singles(l, n, i) + 1 + FREE_SINGLES)
                pe.wait_ge(hid_ready, 2 * CHUNKS * l + CHUNKS * f + j + 2 * i + 1)
                for t in tiles:
                    last = to_output(t, hid_hi[:, j % 2, :], hid_lo[:, j % 2, :], hi_single[:, n % 2, :],
                                     lo_single[:, n % 2, :], False)
                if 1 in tiles:
                    last.then_inc(single_used, 1)

            def finish(l, s, first_rest, second_rest, wait_for):
                for n, operands in enumerate(first_rest):
                    wait_for(n, 0)
                    if n < len(first_rest) - 1:
                        to_output(0, *operands, False)
                    else:
                        for h in range(2):
                            to_output(0, *operands, True, halves=(h,)).then_inc(acc_done, 1)
                wait_for(len(first_rest) - 1, 1)
                operands, used = second_rest[0]
                to_output(1, *operands, False).then_inc(used, 1)
                second_rest = second_rest[1:]
                for h in range(2):
                    for n, (operands, used) in enumerate(second_rest):
                        if h == 1 and n == len(second_rest) - 1:
                            transpose_x(l, s + 1, 0, halves=(0,))
                        last = to_output(1, *operands, n == len(second_rest) - 1, halves=(h,))
                        if h == 1:
                            last.then_inc(used, 1)
                    if h == 0:
                        last.then_inc(acc_done, 1)
                transpose_x(l, s + 1, 0, halves=(1,))

            def last_downs(l, f):
                def operands(j):
                    n = FFN_SINGLE0[f] + j
                    if j == CHUNKS - 1:
                        return last_hid_hi, last_hid_lo, last_hi_single, last_lo_single
                    return hid_hi[:, j % 2, :], hid_lo[:, j % 2, :], hi_single[:, n % 2, :], lo_single[:, n % 2, :]

                def wait_for(m, t):
                    if t == 0:
                        pe.wait_ge(lo_single_ready, singles(l, FFN_SINGLE0[f] + CHUNKS - 2 + m) + 1 + FREE_SINGLES)
                    if m == 0:
                        pe.wait_ge(hid_ready, CHUNKS * (2 * l + f) + CHUNKS - 1)
                    elif t == 0:
                        pe.wait_ge(last_hid_ready, 2 * l + f + 1)
                    else:
                        pe.wait_ge(hid_ready, CHUNKS * (2 * l + f) + CHUNKS)

                finish(l, 2 * f, [operands(CHUNKS - 2), operands(CHUNKS - 1)],
                       [(operands(j), single_used) for j in (CHUNKS - 3, CHUNKS - 2, CHUNKS - 1)], wait_for)

            def to_output(t, y_hi, y_lo, w_hi, w_lo, final, halves=(0, 1)):
                toks = slice(t * P, (t + 1) * P)
                for h in halves:
                    cols = slice(h * HALF, (h + 1) * HALF)
                    last = exact(acc[:, 2 * t + h, :], y_hi[:, toks], y_lo[:, toks], w_hi[:, cols],
                                 w_lo[:, cols], False, final)
                return last

            def ffn(l, f):
                first_chunks(l, f)
                down(l, f, 0)
                with pe.Fori(0, (CHUNKS - 4) // 2) as i:
                    for j in (2, 3):
                        gate_up(l, f, j, i)
                        down(l, f, j - 1, i)
                gate_up(l, f, CHUNKS - 2)
                down(l, f, CHUNKS - 3, tiles=(0,))
                gate_up(l, f, CHUNKS - 1)
                last_downs(l, f)

            nc.tensor.sem_inc(pair_used, FREE_PAIR_TILES)
            nc.tensor.sem_inc(single_used, FREE_SINGLES)
            def keep_busy(count):
                for _ in range(count):
                    nc.tensor.matmul(work[:, 0, 0:SEQ], z_pad[:, 0:P], z_pad[:, 0:SEQ], start=True, stop=True)

            pe.wait_ge(pad_zeroed, 1)
            keep_busy(3)
            pe.wait_ge(ident_landed, 16)
            pe.wait_ge(ident_ready, 1)
            transpose_x(0, 0, 0)
            keep_busy(6)
            with pe.Fori(0, LAYERS) as l:
                ffn(l, 0)

                for t in range(TT):
                    toks = slice(t * P, (t + 1) * P)
                    for g, a in ((0, 0), (0, 1), (1, 0), (1, 1)):
                        n = MIX_PAIR0 + g
                        pe.wait_ge(lo_pair_ready, pair_tiles(l, n) + a + 1 + FREE_PAIR_TILES)
                        for kk in range(2):
                            k = 4 * g + 2 * a + kk
                            if t == 0 and k in (6, 7):
                                transpose_x(l, 1, 1, halves=(k - 6,))
                            spread_done(l, 1, t, k)
                            at = slice(kk * HALF, (kk + 1) * HALF)
                            last = exact(acc[:, t, :], xT_hi[:, k, toks], xT_lo[:, k, toks],
                                         hi_pair[:, n % 2, a, at], lo_pair[:, n % 2, a, at],
                                         k == 0, k == KT - 1)
                        if t == TT - 1:
                            last.then_inc(pair_used, 1)
                for c in range(CT):
                    channels_major(l, MIX_PAIR0 + 2, c, work[:, 0, c * SEQ:(c + 1) * SEQ])

                def gate_b(c):
                    n = MIX_SINGLE0 + c
                    pe.wait_ge(lo_single_ready, singles(l, n) + 1 + FREE_SINGLES)
                    for k in range(KT):
                        at = slice(k * P, (k + 1) * P)
                        last = exact(work[:, 2, c * SEQ:(c + 1) * SEQ], hi_single[:, n % 2, at],
                                     lo_single[:, n % 2, at], xT_hi[:, k, :], xT_lo[:, k, :],
                                     k == 0, k == KT - 1)
                    last.then_inc(single_used, 1)

                channels_major(l, MIX_PAIR0 + 3, 0, work[:, 1, 0:SEQ])
                channels_major(l, MIX_PAIR0 + 3, 1, work[:, 1, SEQ:2 * SEQ])
                gate_b(0)
                pe.wait_ge(const_landed, 16 * CONST_LOADS)
                for q in range(2):
                    pe.wait_ge(a_folded, 2 * l + q + 1)
                    for c in range(CT):
                        last = nc.tensor.matmul(acc[:, TT + q, c * 2 * P:(c + 1) * 2 * P],
                                                a_fold[:, q, c, :], dft_ch[:, :], start=True, stop=True)
                    last.then_inc(dft1_done, 1)
                channels_major(l, MIX_PAIR0 + 4, 0, work[:, 3, 0:SEQ])
                channels_major(l, MIX_PAIR0 + 4, 1, work[:, 3, SEQ:2 * SEQ])
                pe.wait_ge(yc_ready, CT * l + 1)
                gate_b(1)
                pe.wait_ge(p_ready, TT * (l + 1))
                for g in range(HEADS):
                    dst = work[(g % 2) * HEAD:(g % 2 + 1) * HEAD, 0, (g // 2) * SEQ:(g // 2 + 1) * SEQ]
                    for t in range(TT):
                        to = slice(0, P + POOL_REACH) if t == 0 else slice(P - POOL_REACH, SEQ)
                        last = nc.tensor.matmul(dst[:, to], p_tok[:, t, g * HEAD:(g + 1) * HEAD],
                                                pool_m[:, g, t, :], start=(t == 0), stop=(t == TT - 1),
                                                skip_group_check=True)
                last.then_inc(pool_done, 1)
                pe.wait_ge(v_ready, TT * (l + 1))
                pe.wait_ge(params_landed, 16 * PARAM_LOADS * (l + 1))
                for g in range(HEADS):
                    for t in range(TT):
                        col = (g // 2) * SEQ + t * P
                        dst = acc[(g % 2) * HEAD:(g % 2 + 1) * HEAD, 0, col:col + P]
                        last = nc.tensor.matmul(dst, v_tok[:, t, g * HEAD:(g + 1) * HEAD], ws[:, g, :],
                                                start=True, stop=True)
                last.then_inc(spatial_done, 1)
                pe.wait_ge(y1_ready, 2 * (l + 1))
                for c in range(CT):
                    for q in range(2):
                        dst = acc[:, 1, c * SEQ + q * P:c * SEQ + (q + 1) * P]
                        for trig in range(2):
                            col = c * 2 * P + trig * P
                            last = nc.tensor.matmul(dst, y1[:, q, col:col + P], dft_tok[:, trig, q, :],
                                                    start=(trig == 0), stop=(trig == 1))
                last.then_inc(dft2_done, 1)
                pe.wait_ge(z_ready, CT * l + 1)
                for c in range(CT):
                    channels_major(l, MIX_PAIR0 + 5, c, work[:, 1, c * SEQ:(c + 1) * SEQ])
                pe.wait_ge(pooled_ready, l + 1)
                pe.wait_ge(z_ready, CT * (l + 1))
                for c in range(CT):
                    last = nc.tensor.matmul(work[:, 3, c * SEQ:(c + 1) * SEQ], pool_bd[:, c, :],
                                            pooled[:, c, :], start=True, stop=True)
                last.then_inc(pool_w_done, 1)
                pe.wait_ge(mixed_ready, CT * (l + 1))
                pe.wait_ge(ya_ready, CT * (l + 1))
                residual(l, 1)

                def out_tile(g, a, k):
                    n = MIX_PAIR0 + g
                    return yT_hi[:, k, :], yT_lo[:, k, :], hi_pair[:, n % 2, a, :], lo_pair[:, n % 2, a, :]

                def out_tile_ready(g, a):
                    pe.wait_ge(lo_pair_ready, pair_tiles(l, MIX_PAIR0 + g) + a + 1 + FREE_PAIR_TILES)

                def out_single(g, k):
                    n = MIX_SINGLE0 + g
                    return yT_hi[:, k, :], yT_lo[:, k, :], hi_single[:, n % 2, :], lo_single[:, n % 2, :]

                def out_single_ready(g):
                    pe.wait_ge(lo_single_ready, singles(l, MIX_SINGLE0 + g) + 1 + FREE_SINGLES)

                def both_tokens(operands, used):
                    for t in range(TT):
                        last = to_output(t, *operands, False)
                    last.then_inc(used, 1)

                for a in range(2):
                    out_tile_ready(6, a)
                    both_tokens(out_tile(6, a, a), pair_used)
                pe.wait_ge(yc_ready, CT * (l + 1))
                for g, k in ((2, 4), (3, 5)):
                    out_single_ready(g)
                    both_tokens(out_single(g, k), single_used)
                pe.wait_ge(yb_ready, l + 1)
                out_tile_ready(7, 0)
                both_tokens(out_tile(7, 0, 2), pair_used)

                def wait_for(m, t):
                    if t == 0:
                        if m == 0:
                            out_tile_ready(7, 1)
                        else:
                            pe.wait_ge(yd_ready, l + 1)
                            out_single_ready(m + 3)

                finish(l, 1, [out_tile(7, 1, 3), out_single(4, 6), out_single(5, 7)],
                       [(out_tile(7, 1, 3), pair_used), (out_single(4, 6), single_used),
                        (out_single(5, 7), single_used)], wait_for)

                ffn(l, 1)


def constants():
    n = np.arange(HEAD)
    ang = 2 * np.pi * np.outer(n, n) / HEAD
    ch = np.zeros((P, 2, 2, HEAD))
    for hh in range(2):
        ch[hh * HEAD:(hh + 1) * HEAD, 0, hh] = np.cos(ang)
        ch[hh * HEAD:(hh + 1) * HEAD, 1, hh] = np.sin(ang)
    ch = ch.reshape(P, 2 * P) / np.sqrt(HEAD)
    assert SEQ == 2 * P
    ang = 2 * np.pi * (np.outer(np.arange(P), np.arange(SEQ)) % SEQ) / SEQ
    tok = np.stack([np.cos(ang), -np.sin(ang)]) / np.sqrt(SEQ)
    tok = tok.reshape(2, P, P, 2).transpose(1, 0, 3, 2)
    pool = np.zeros((HEADS, SEQ, SEQ))
    for g, w in enumerate(WINDOWS):
        for t in range(SEQ):
            lo, hi = max(t - w // 2, 0), min(t + w - w // 2, SEQ)
            pool[g, lo:hi, t] = 1.0 / (hi - lo)
            pool[g, t, t] -= 1.0
    pool = pool.reshape(HEADS, TT, P, SEQ)
    pool = np.stack([pool[:, 0, :, :P + POOL_REACH], pool[:, 1, :, P - POOL_REACH:]], axis=1).transpose(2, 0, 1, 3)
    return {"ident": np.eye(P), "dft_channels": ch, "dft_tokens": tok, "pool_matrix": pool}


def kernel(**inputs):
    import concourse.bacc as bacc
    from concourse.bass_utils import run_bass_kernel_spmd as run

    a = {k: np.asarray(v) for k, v in inputs.items()}
    L, C = LAYERS, CHUNKS

    def columns(w, tile):
        n = w.shape[2] // tile
        return w.reshape(L, KT, P, n, tile).transpose(0, 3, 2, 1, 4)

    def ffn_pairs(n):
        gate = columns(a[f"ffn{n}_w_gate"], P).reshape(L * C, P, W)
        up = columns(a[f"ffn{n}_w_up"], P).reshape(L * C, P, W)
        return np.concatenate([gate, up], axis=2)

    w_in, w_out = a["mix_w_in"], a["mix_w_out"].reshape(L, KT, P, D)
    part = [w_in[:, :, i * GROUP:(i + 1) * GROUP] for i in range(7)]
    wa, wp, wb, wc, wh, wu, wv = part
    pv = np.concatenate([wp, wv], axis=2).reshape(L, 2, 4, P, 2 * GROUP).transpose(0, 1, 3, 2, 4)
    pv = pv.reshape(L, 2, P, 2 * W)
    ta, tb, tc, th, tu = [columns(w, P).reshape(L, CT, P, W) for w in (wa, wb, wc, wh, wu)]

    def pair(m, n):
        return np.concatenate([m, n], axis=2)

    mix_pairs = np.stack([
        pv[:, 0], pv[:, 1], pair(ta[:, 0], ta[:, 1]), pair(tc[:, 0], th[:, 0]), pair(tc[:, 1], th[:, 1]),
        pair(tu[:, 0], tu[:, 1]), pair(w_out[:, 0], w_out[:, 1]), pair(w_out[:, 2], w_out[:, 3])], axis=1)
    mix_singles = np.stack([tb[:, 0], tb[:, 1], w_out[:, 4], w_out[:, 5], w_out[:, 6], w_out[:, 7]], axis=1)
    conv = a["conv_w"].reshape(L, 3, CT, P).transpose(0, 3, 1, 2)
    small = np.concatenate([a["pool_scale"].reshape(L, 1, CT, P).transpose(0, 3, 1, 2), conv], axis=2)

    def by_parity(w):
        return w.reshape(L, CT, 2, *w.shape[2:])

    arrays = {
        "x": a["x"].reshape(SEQ, D),
        "ffn_pairs": np.concatenate([ffn_pairs(1), ffn_pairs(2)]),
        "ffn_singles": np.stack([a["ffn1_w_down"].reshape(L * C, P, D), a["ffn2_w_down"].reshape(L * C, P, D)]),
        "mix_pairs": mix_pairs.reshape(L * MIX_PAIRS, P, 2 * W),
        "mix_singles": mix_singles.reshape(L * MIX_SINGLES, P, W),
        "ln_params": np.stack([a[f"ln{s}_{w}"] for s in (1, 2, 3) for w in "gb"], axis=1),
        "v_params": np.stack([a["gmlp_ln_g"], a["gmlp_ln_b"]], axis=1),
        "gate_bias": by_parity(a["gmlp_b_s"]).transpose(0, 2, 1, 3),
        "pool_w": by_parity(a["pool_w"]).transpose(0, 2, 3, 1, 4),
        "small": small.reshape(L, P, 4 * CT),
        "spatial_w": a["gmlp_w_s"].transpose(0, 3, 1, 2),
        **constants(),
    }
    nc = bacc.Bacc("TRN2", target_bir_lowering=False, num_devices=1)
    sent, args = {}, []
    for name, v in arrays.items():
        v = np.ascontiguousarray(v, dtype=np.float32)
        sent[name + "_dram"] = v
        args.append(nc.dram_tensor(name + "_dram", v.shape, F32, kind="ExternalInput").ap())
    args.append(nc.dram_tensor("out_dram", (SEQ, D), F32, kind="ExternalOutput").ap())
    build(nc, *args)
    r = run(nc, [sent], core_ids=[0])
    return r.results[0]["out_dram"].reshape(1, SEQ, D)
```
